# Optimizing a Trainium2 kernel written in Bass

```python
import math
import jax, jax.numpy as jnp
from jax import lax
import numpy as np

"""Hybrid diffusion backbone trunk (4 layers) over latent tokens with an un-noised context prefix.

Inputs:  x (BATCH, SEQ, D_MODEL) latent tokens, c (BATCH, D_MODEL) conditioning vector,
         ctx (BATCH, CTX_LEN, D_MODEL) context tokens, c_ctx (D_MODEL,) context modulation vector,
         plus per-layer stacked weights and a router shared by all layers.
Output:  (BATCH, SEQ, D_MODEL) final-RMSNorm'd latent stream.

Per layer (same weights for context and latent tokens):
  adaLN-modulated RMSNorm -> ONE combined input projection whose columns are split into
  three parallel head groups (chunked gMLP spatial gating | short gated conv | windowed GQA
  with sink + 2-D axial rotary, latent queries also read all context keys) -> concat -> ONE
  output projection -> gated residual; then adaLN-modulated RMSNorm -> grouped top-2 MoE
  with a router shared across layers -> gated residual.
"""

D_MODEL = 1024
BATCH = 1
SEQ = 256
DEPTH = 2

CTX_LEN = 256
GRID_W = 64

W_A = D_MODEL // 4
A_GROUPS = 4
A_CHUNK = 128
W_B = D_MODEL // 4
CONV_W = 3
HEAD_DIM = 64
W_C = D_MODEL // 2
N_HEADS = W_C // HEAD_DIM
N_KV = 2
WINDOW = 128
BLOCK = 128
MIX_WIDTH = W_A + W_B + W_C
ROPE_BASE = 10000.0
QUARTER = HEAD_DIM // 4
ATTN_SCALE = HEAD_DIM ** -0.5
EPS = 1e-6

SPLITS = (W_A, 2 * W_A, 2 * W_A + W_B, 2 * W_A + 2 * W_B, 2 * W_A + 3 * W_B,
          2 * W_A + 3 * W_B + W_C, 2 * W_A + 3 * W_B + W_C + N_KV * HEAD_DIM)
KV_START = 2 * W_A + 3 * W_B + W_C
IN_COLS = KV_START + 2 * N_KV * HEAD_DIM

N_EXPERTS = 16
N_GROUPS = 4
EXPERTS_PER_GROUP = N_EXPERTS // N_GROUPS
TOP_K = 2
D_EXPERT = 512

kernel_name = "hybrid_parallel_mixer_diffusion_trunk"

def rms_norm(x, g):
    xf = x.astype(jnp.float32)
    y = xf * lax.rsqrt(jnp.mean(xf * xf, axis=-1, keepdims=True) + EPS)
    return (y * g.astype(jnp.float32)).astype(x.dtype)

def modulation(cvec, w_mod, b_mod):
    m = (jax.nn.silu(cvec) @ w_mod + b_mod)[:, None, :]
    return jnp.split(m, 6, axis=-1)

def axial_rope_tables(n, dtype):
    rows = n // GRID_W
    row = jnp.repeat(jnp.arange(rows, dtype=jnp.float32), GRID_W)
    col = jnp.tile(jnp.arange(GRID_W, dtype=jnp.float32), rows)
    inv = ROPE_BASE ** (-jnp.arange(QUARTER, dtype=jnp.float32) / QUARTER)
    ang = jnp.stack([row[:, None] * inv, col[:, None] * inv], axis=1)
    ang = ang[:, None]
    return jnp.cos(ang).astype(dtype), jnp.sin(ang).astype(dtype)

def apply_axial_rope(t, cos, sin):
    tr = t.reshape(t.shape[:-1] + (2, 2, QUARTER))
    t1, t2 = tr[..., 0, :], tr[..., 1, :]
    o1 = t1 * cos - t2 * sin
    o2 = t2 * cos + t1 * sin
    return jnp.stack([o1, o2], axis=-2).reshape(t.shape)

def chunk_gmlp(u, v, g_v, w_s, b_s):
    b_, n, _ = u.shape
    u = jax.nn.gelu(u)
    v = rms_norm(jax.nn.gelu(v), g_v)
    v = v.reshape(b_, n // A_CHUNK, A_CHUNK, A_GROUPS, W_A // A_GROUPS)
    s = jnp.einsum('hpq,bcqhd->bcphd', w_s, v) + b_s.T[None, None, :, :, None]
    return u * s.reshape(b_, n, W_A)

def short_gated_conv(bg, cg, h, w_conv):
    z = cg * h
    n = z.shape[1]
    zp = jnp.pad(z, ((0, 0), (1, 1), (0, 0)))
    y = zp[:, :n] * w_conv[0] + zp[:, 1:n + 1] * w_conv[1] + zp[:, 2:] * w_conv[2]
    return bg * y

def context_attention(q, k, v, sink):
    b_, L = q.shape[:2]
    g = N_HEADS // N_KV
    qg = q.reshape(b_, L, N_KV, g, HEAD_DIM)
    s = jnp.einsum('bqkgd,bskd->bkgqs', qg, k, preferred_element_type=jnp.float32) * ATTN_SCALE
    s_sink = jnp.broadcast_to(sink.astype(jnp.float32).reshape(1, N_KV, g, 1, 1), s.shape[:-1] + (1,))
    p = jax.nn.softmax(jnp.concatenate([s, s_sink], axis=-1), axis=-1)[..., :L].astype(v.dtype)
    o = jnp.einsum('bkgqs,bskd->bqkgd', p, v)
    return o.reshape(b_, L, N_HEADS * HEAD_DIM)

def window_attention(q, k, v, k_ctx, v_ctx, sink):
    b_, n = q.shape[:2]
    nb = n // BLOCK
    g = N_HEADS // N_KV
    L = k_ctx.shape[1]
    nl = 3 * BLOCK
    qb = q.reshape(b_, nb, BLOCK, N_KV, g, HEAD_DIM)

    def band(t):
        tp = jnp.pad(t.reshape(b_, nb, BLOCK, N_KV, HEAD_DIM), ((0, 0), (1, 1), (0, 0), (0, 0), (0, 0)))
        return jnp.concatenate([tp[:, :-2], tp[:, 1:-1], tp[:, 2:]], axis=2)

    kb, vb = band(k), band(v)
    s_loc = jnp.einsum('bnqkgd,bnskd->bnkgqs', qb, kb, preferred_element_type=jnp.float32) * ATTN_SCALE
    blk = jnp.arange(nb)[:, None, None]
    qpos = blk * BLOCK + jnp.arange(BLOCK)[None, :, None]
    kpos = (blk - 1) * BLOCK + jnp.arange(nl)[None, None, :]
    valid = (jnp.abs(qpos - kpos) <= WINDOW) & (kpos >= 0) & (kpos < n)
    s_loc = jnp.where(valid[None, :, None, None], s_loc, -jnp.inf)
    s_ctx = jnp.einsum('bnqkgd,bskd->bnkgqs', qb, k_ctx, preferred_element_type=jnp.float32) * ATTN_SCALE
    s_sink = jnp.broadcast_to(sink.astype(jnp.float32).reshape(1, 1, N_KV, g, 1, 1), s_ctx.shape[:-1] + (1,))
    p = jax.nn.softmax(jnp.concatenate([s_loc, s_ctx, s_sink], axis=-1), axis=-1).astype(v.dtype)
    o = (jnp.einsum('bnkgqs,bnskd->bnqkgd', p[..., :nl], vb)
         + jnp.einsum('bnkgqs,bskd->bnqkgd', p[..., nl:nl + L], v_ctx))
    return o.reshape(b_, n, N_HEADS * HEAD_DIM)

def grouped_moe(h, router_w, router_b, w_gate, w_up, w_down):
    n = h.shape[0]
    scores = jax.nn.sigmoid(jnp.einsum('nd,de->ne', h, router_w, preferred_element_type=jnp.float32))
    sel = (scores + router_b.astype(jnp.float32)).reshape(n, N_GROUPS, EXPERTS_PER_GROUP)
    group_score = jnp.sum(lax.top_k(sel, TOP_K)[0], axis=-1)
    best_group = jnp.argmax(group_score, axis=-1)
    in_group = jnp.take_along_axis(sel, best_group[:, None, None], axis=1)[:, 0]
    _, top_idx = lax.top_k(in_group, TOP_K)
    expert_idx = best_group[:, None] * EXPERTS_PER_GROUP + top_idx
    w = jnp.take_along_axis(scores, expert_idx, axis=-1)
    w = w / jnp.sum(w, axis=-1, keepdims=True)
    gates = jnp.sum(jax.nn.one_hot(expert_idx, N_EXPERTS, dtype=jnp.float32) * w[..., None], axis=1).astype(h.dtype)
    out = jnp.zeros_like(h)
    for e in range(N_EXPERTS):
        a = jax.nn.silu(h @ w_gate[e]) * (h @ w_up[e])
        out = out + gates[:, e:e + 1] * (a @ w_down[e])
    return out

def trunk_layer(x, xc, mod_x, mod_c, norm1_g, norm2_g, w_in, gmlp_g, w_s, b_s, conv_w, sink,
                w_out, router_w, router_b, w_gate, w_up, w_down, cos, sin, ctx_out):
    b_, n, d = x.shape
    L = xc.shape[1]
    sh1, sc1, g1, sh2, sc2, g2 = mod_x
    csh1, csc1, cg1, csh2, csc2, cg2 = mod_c

    hx = rms_norm(x, norm1_g) * (1 + sc1) + sh1
    hc = rms_norm(xc, norm1_g) * (1 + csc1) + csh1
    ux, vx, bx, cx, zx, qx, kx, vvx = jnp.split(hx @ w_in, SPLITS, axis=-1)
    qx = apply_axial_rope(qx.reshape(b_, n, N_HEADS, HEAD_DIM), cos, sin)
    kx = apply_axial_rope(kx.reshape(b_, n, N_KV, HEAD_DIM), cos, sin)
    vvx = vvx.reshape(b_, n, N_KV, HEAD_DIM)
    if ctx_out:
        uc, vc, bc, cc, zc, qc, kc, vvc = jnp.split(hc @ w_in, SPLITS, axis=-1)
    else:
        kc, vvc = jnp.split(hc @ w_in[:, KV_START:], 2, axis=-1)
    kc = kc.reshape(b_, L, N_KV, HEAD_DIM)
    vvc = vvc.reshape(b_, L, N_KV, HEAD_DIM)

    mix_x = jnp.concatenate([
        chunk_gmlp(ux, vx, gmlp_g, w_s, b_s),
        short_gated_conv(bx, cx, zx, conv_w),
        window_attention(qx, kx, vvx, kc, vvc, sink)], axis=-1) @ w_out
    x = x + g1 * mix_x
    if ctx_out:
        mix_c = jnp.concatenate([
            chunk_gmlp(uc, vc, gmlp_g, w_s, b_s),
            short_gated_conv(bc, cc, zc, conv_w),
            context_attention(qc.reshape(b_, L, N_HEADS, HEAD_DIM), kc, vvc, sink)], axis=-1) @ w_out
        xc = xc + cg1 * mix_c

    h2x = rms_norm(x, norm2_g) * (1 + sc2) + sh2
    if ctx_out:
        h2c = rms_norm(xc, norm2_g) * (1 + csc2) + csh2
        tokens = jnp.concatenate([h2x.reshape(-1, d), h2c.reshape(-1, d)], axis=0)
        y = grouped_moe(tokens, router_w, router_b, w_gate, w_up, w_down)
        x = x + g2 * y[:b_ * n].reshape(b_, n, d)
        xc = xc + cg2 * y[b_ * n:].reshape(b_, L, d)
    else:
        y = grouped_moe(h2x.reshape(-1, d), router_w, router_b, w_gate, w_up, w_down)
        x = x + g2 * y.reshape(b_, n, d)
    return x, xc

def setup_inputs(seed: int = 0) -> dict:
    key = jax.random.key(seed)
    ks = jax.random.split(key, 24)
    f32 = jnp.float32

    def nrm(k, shape, s):
        return jax.random.normal(k, shape, f32) * s

    return {
        "x": nrm(ks[0], (BATCH, SEQ, D_MODEL), 1.0),
        "c": nrm(ks[1], (BATCH, D_MODEL), 1.0),
        "ctx": nrm(ks[2], (BATCH, CTX_LEN, D_MODEL), 1.0),
        "c_ctx": nrm(ks[3], (D_MODEL,), 1.0),
        "w_mod": nrm(ks[4], (DEPTH, D_MODEL, 6 * D_MODEL), 0.5 * D_MODEL ** -0.5),
        "b_mod": nrm(ks[5], (DEPTH, 6 * D_MODEL), 0.02),
        "norm1_g": 1.0 + nrm(ks[6], (DEPTH, D_MODEL), 0.02),
        "norm2_g": 1.0 + nrm(ks[7], (DEPTH, D_MODEL), 0.02),
        "w_in": nrm(ks[8], (DEPTH, D_MODEL, IN_COLS), D_MODEL ** -0.5),
        "gmlp_g": 1.0 + nrm(ks[9], (DEPTH, W_A), 0.02),
        "w_s": nrm(ks[10], (DEPTH, A_GROUPS, A_CHUNK, A_CHUNK), A_CHUNK ** -0.5),
        "b_s": nrm(ks[11], (DEPTH, A_GROUPS, A_CHUNK), 0.02),
        "conv_w": nrm(ks[12], (DEPTH, CONV_W, W_B), CONV_W ** -0.5),
        "attn_sink": nrm(ks[13], (DEPTH, N_HEADS), 0.5),
        "w_out": nrm(ks[14], (DEPTH, MIX_WIDTH, D_MODEL), MIX_WIDTH ** -0.5),
        "router_w": nrm(ks[15], (D_MODEL, N_EXPERTS), D_MODEL ** -0.5),
        "router_b": nrm(ks[16], (N_EXPERTS,), 0.01),
        "w_gate": nrm(ks[17], (DEPTH, N_EXPERTS, D_MODEL, D_EXPERT), D_MODEL ** -0.5),
        "w_up": nrm(ks[18], (DEPTH, N_EXPERTS, D_MODEL, D_EXPERT), D_MODEL ** -0.5),
        "w_down": nrm(ks[19], (DEPTH, N_EXPERTS, D_EXPERT, D_MODEL), D_EXPERT ** -0.5),
        "final_g": 1.0 + nrm(ks[20], (D_MODEL,), 0.02),
    }

def reference(x, c, ctx, c_ctx, w_mod, b_mod, norm1_g, norm2_g, w_in, gmlp_g, w_s, b_s, conv_w,
              attn_sink, w_out, router_w, router_b, w_gate, w_up, w_down, final_g):
    n = x.shape[1]
    cos, sin = axial_rope_tables(n, x.dtype)
    xc = ctx
    for layer in range(DEPTH):
        mod_x = modulation(c, w_mod[layer], b_mod[layer])
        mod_c = modulation(c_ctx[None], w_mod[layer], b_mod[layer])
        x, xc = trunk_layer(x, xc, mod_x, mod_c, norm1_g[layer], norm2_g[layer], w_in[layer],
                            gmlp_g[layer], w_s[layer], b_s[layer], conv_w[layer], attn_sink[layer],
                            w_out[layer], router_w, router_b, w_gate[layer], w_up[layer], w_down[layer],
                            cos, sin, layer < DEPTH - 1)
    return rms_norm(x, final_g)


_drawn_inputs = setup_inputs


def setup_inputs(seed=0):
    import zlib

    import numpy as np

    out = dict(_drawn_inputs(seed))
    spreads = {}
    factors = {'gmlp_g': 6.049, 'b_s': 8.0, 'attn_sink': 21.756, 'final_g': 8.779}
    for name, (base, spread) in spreads.items():
        noise = np.random.default_rng([zlib.crc32(name.encode()), seed]).standard_normal(out[name].shape)
        drawn = base * np.exp(spread * noise) if base else spread * noise
        out[name] = __import__('jax').numpy.asarray(drawn.astype(out[name].dtype))
    for name, factor in factors.items():
        out[name] = (out[name] * factor).astype(out[name].dtype)
    return out
```

```python
from contextlib import ExitStack

import numpy as np

import concourse.bass as bass
from concourse import mybir

F32 = mybir.dt.float32
I32 = mybir.dt.int32
U32 = mybir.dt.uint32
ALU = mybir.AluOpType
ACT = mybir.ActivationFunctionType
AX = mybir.AxisListType.X

P = 128
MB = 1 << 20
EPS = 1e-6
GRID_W = 64
ROPE_BASE = 10000.0
SLOTS = 64
RING = 3
MASKED = -1e30

C_ID, C_COS, C_SIN, C_MASK, C_FOLD, C_COUNT = 0, 128, 256, 384, 640, 656
N_CONST = 664
R_BEFORE, R_ONES, R_PREFIX = 0, 128, 256


def shape_constants(head_dim):
    quarter = head_dim // 4
    tok = np.arange(2 * P, dtype=np.float32)
    inv = (ROPE_BASE ** (-np.arange(quarter, dtype=np.float32) / quarter)).astype(np.float32)
    ang = np.stack([np.floor(tok / GRID_W)[:, None] * inv, (tok % GRID_W)[:, None] * inv], axis=1)
    cos, sin = np.cos(ang), np.sin(ang)
    cos2 = np.stack([cos, cos], axis=2).reshape(2, P, head_dim)
    sin2 = np.stack([-sin, sin], axis=2).reshape(2, P, head_dim)
    i, j = np.arange(P)[:, None], np.arange(P)[None, :]
    consts = np.concatenate([
        np.eye(P), cos2[0], cos2[1], sin2[0], sin2[1],
        np.where(j > i, MASKED, 0.0), np.where(i > j, MASKED, 0.0),
        (i % 32 == np.arange(16)), np.tile(np.arange(8), (P, 1)),
    ], axis=1).astype(np.float32)
    return consts


def router_constants(n_experts):
    i, j = np.arange(P)[:, None], np.arange(P)[None, :]
    before = (np.arange(n_experts)[None, :] < np.arange(n_experts + 1)[:, None]).reshape(1, -1)
    return np.concatenate([i < j, np.ones((P, P)), np.tile(before, (P, 1))], axis=1).astype(np.float32)


class Stage:

    def __init__(self, sem, total):
        self.sem, self.total = sem, total

    def at(self, layer, n):
        return layer * self.total + n


class Window:

    def __init__(self, eng, limit):
        self.eng, self.limit, self.flying = eng, limit, []

    def room(self, nbytes):
        while self.flying and sum(n for n, _, _ in self.flying) + nbytes > self.limit:
            _, sem, value = self.flying.pop(0)
            self.eng.wait_ge(sem, value)

    def started(self, nbytes, sem, value):
        self.flying.append((nbytes, sem, value))


class Tally:

    def __init__(self, eng, sem):
        self.eng, self.sem, self.n = eng, sem, 0

    def inc(self, ins):
        ins.then_inc(self.sem, 1)
        self.n += 1
        return self.n

    def link(self, ins):
        self.eng.wait_ge(self.sem, self.inc(ins))


def hybrid_trunk(nc, x, c, ctx, c_ctx, w_mod, b_mod, norm1_g, norm2_g, w_in, gmlp_g, w_s, b_s,
                 conv_w, attn_sink, w_out, router_w, router_b, w_gate, w_up, w_down, final_g,
                 consts, rconsts, out):
    DEPTH, D, _ = w_mod.shape
    KD = D // P
    W_A = gmlp_g.shape[1]
    A_GROUPS = w_s.shape[1]
    NH = attn_sink.shape[1]
    HD = 64
    NKV = 2
    W_C = NH * HD
    W_B = conv_w.shape[2]
    COL_U, COL_V, COL_B, COL_C, COL_Z = 0, W_A, 2 * W_A, 2 * W_A + W_B, 2 * W_A + 2 * W_B
    COL_Q = 2 * W_A + 3 * W_B
    COL_K = COL_Q + W_C
    IN_COLS = w_in.shape[2]
    KV2 = IN_COLS - COL_K
    SCALE = HD ** -0.5
    NE = w_gate.shape[1]
    FE = w_gate.shape[3]
    KF = FE // P
    NX, NALL = 2, 4
    MODW = 6 * D
    NTILE = 2 * NALL * P // SLOTS + NE
    NP = 6 * DEPTH
    HK = KD // 2
    MQ = D // 4
    FIRST = 4
    NT = [NALL if l < DEPTH - 1 else NX for l in range(DEPTH)]

    es = ExitStack()
    with es:
        def sb(name, shape, dt=F32):
            return es.enter_context(nc.sbuf_tensor(name, shape, dt))

        def sem(name):
            return es.enter_context(nc.semaphore(name))

        def lsem(name):
            return [sem(f"{name}_{l}") for l in range(DEPTH)]

        mod_d = nc.dram_tensor("mod_rows", [DEPTH, 2, MODW], F32).ap()
        hsort = nc.dram_tensor("h_by_expert", [NTILE * SLOTS, D], F32).ap()
        ysort = nc.dram_tensor("y_by_expert", [NTILE * SLOTS, D], F32).ap()

        SLOT = 2 * KD * FE + KF * D
        big = sb("weight_ring", [P, RING * SLOT])
        xres = sb("residual", [P, NALL, D])
        ybuf = sb("conv_y", [P, D])
        vbuf = sb("gmlp_v", [P, D])
        qkbuf = sb("qk_tokens", [P, NALL * (W_C + 256) + NALL * P])
        qtbuf = sb("q_k_transposed", [P, 4096])
        cst = sb("consts_sb", [P, N_CONST])
        mrow = sb("modulation_sums", [P, MQ])
        esum = sb("sink_minus_max", [P, NH])
        wst = sb("w_s_transposed", [P, A_GROUPS, P])
        bsb = sb("b_s_rows", [P, 2, P])
        gvb = sb("gmlp_g_rows", [P, W_A])
        rwb = sb("router_w_sb", [P, KD, NE])
        mt = sb("modulation_columns", [P, P])
        a1t = sb("norm1_scale", [P, 2, KD])
        sinkb = sb("sink_rows", [P, NH])
        nsink = sb("minus_sink", [P, NH])
        rbb = sb("router_b_rows", [P, NE])
        st = sb("row_stats", [P, 6, NALL + 1])
        mx = sb("score_max", [P, NH])
        nmx = sb("minus_max", [P, 2, NH])
        rsum = sb("prob_sum", [P, 2, NH])
        esink = sb("sink_prob", [P, NH])
        rden = sb("inverse_sum", [P, NH])
        posf = sb("slot_numbers_f", [P, 2, NALL])
        posi = sb("slot_numbers", [P, 2, NALL], I32)
        wtk = sb("gate_weights", [P, 2, NALL])
        tab = [sb(f"first_tile_{l}", [1, 32], I32) for l in range(DEPTH)]

        def slot(n, a=0, m=SLOT):
            return big[:, (n % RING) * SLOT + a:(n % RING) * SLOT + a + m]

        def wgate(n):
            return slot(n, 0, KD * FE).rearrange("p (k f) -> p k f", k=KD)

        def wup(n):
            return slot(n, KD * FE, KD * FE).rearrange("p (k f) -> p k f", k=KD)

        def wdown(n):
            return slot(n, 2 * KD * FE, KF * D).rearrange("p (k f) -> p k f", k=KF)

        def win(l, kind):
            off, n = KD * win_at[kind], cols_of[kind][1]
            return big[:, l * SLOT + off:l * SLOT + off + KD * n].rearrange("p (k f) -> p k f", k=KD)

        def wout(l):
            a = l * SLOT + KD * IN_COLS
            return big[:, a:a + KD * D].rearrange("p (k f) -> p k f", k=KD)

        def work(l, a, m):
            return slot(l + 2, a, m)

        def ht(l):
            return work(l, 0, 4096).rearrange("p (k t) -> p k t", k=KD)

        def mixt(l):
            return work(l, 4096, 4096).rearrange("p (k t) -> p k t", k=KD)

        def cz(l):
            return work(l, 8192, 1024).rearrange("p (j t) -> p j t", j=2)

        def ropet(l):
            return work(l, 9216, 768)

        sct = work(0, 9984, 256).rearrange("p (k m) -> p k m", k=KD)

        def hr(l, i):
            return work(l, 10240 + 1024 * i, 1024)

        def prob(l, i):
            return work(l, 10240 + 512 * i, 512)

        def probt(l, i):
            return work(l, 11264 + 512 * i, 512).rearrange("p (k q) -> p k q", k=4)

        def wmodbuf(m):
            a = KD * IN_COLS + (m % 2) * HK * D if m not in (2, 3) else 2 * SLOT + (m % 2) * HK * D
            return big[:, a:a + HK * D].rearrange("p (k n) -> p k n", k=HK)

        def ybuf2(t, k):
            a = 4096 + 1024 * (2 * (t % 3) + k)
            return big[:, a:a + 1024]

        rt0 = 8192

        def chosen_experts(l):
            return work(l, rt0 + 896, (NALL + 1) * NE)

        def logit_quarters(l):
            return work(l, 9744, P)

        QW = W_C + 256
        qk = qkbuf[:, 0:NALL * QW].rearrange("p (t n) -> p t n", t=NALL)
        vv = qkbuf[:, NALL * QW:NALL * QW + NALL * P].rearrange("p (t n) -> p t n", t=NALL)
        vt = vbuf[:, :].rearrange("p (t n) -> p t n", t=NALL)
        yc = ybuf[:, :].rearrange("p (j t) -> p j t", j=2)
        rows = qtbuf[:, 0:P]
        ws_raw = qtbuf[:, P:P + 512].rearrange("p (h q) -> p h q", h=A_GROUPS)
        qT = qtbuf[:, 0:2048].rearrange("p (b t) -> p b t", b=4)
        kz = qtbuf[:, 2048:4096].rearrange("p (z v t) -> p z v t", z=2, v=NKV)
        h2 = qtbuf[:, :].rearrange("p (t n) -> p t n", t=NALL)
        hrow = qkbuf[0:SLOTS, 0:1024]
        hTe = qkbuf[:, 1024:1536].rearrange("p (k s) -> p k s", k=KD)
        sg = qkbuf[SLOTS:P, 1536:2048]
        ae = qkbuf[0:SLOTS, 2048:2560]
        aTe = qkbuf[:, 2560:2816].rearrange("p (k s) -> p k s", k=KF)
        ysb = qkbuf[:, 2816:3328]
        ident = cst[:, C_ID:C_ID + P]

        pb = [es.enter_context(nc.psum_tensor(f"bank{i}", [P, 512], F32)) for i in range(8)]

        s_const = sem('s_const')
        s_cvec = sem('s_cvec')
        s_x = [sem('s_x'), sem('s_ctx')]
        s_sctz = sem('s_sct_zeroed')
        s_ctp = sem('s_c_transposed')
        s_sct = sem('s_sct')
        s_wm = [sem(f"s_wmod_{i}") for i in range(4)]
        s_binit, s_modpe, s_mr, s_modw = sem("s_bmod_rows"), sem("s_modpe"), sem("s_modcopied"), sem("s_modstored")
        s_esum = Stage(sem("s_sink_minus_max"), 4)
        s_row = Stage(sem("s_rows"), 48)
        s_small = Stage(sem("s_small"), 112)
        s_mtp = Stage(sem("s_mtp"), 1)
        s_mt = Stage(sem("s_mt"), 1)
        s_wsp = Stage(sem("s_wsp"), 1)
        s_wst = Stage(sem("s_wst"), 1)
        s_ss = Stage(sem("s_ss"), 4)
        s_hr = Stage(sem("s_hr"), 4)
        s_ta = Stage(sem("s_ta"), 8)
        s_tA = Stage(sem("s_tA"), 4)
        s_tV = Stage(sem("s_tV"), 4)
        GROUPS = ['q', 'kv', 'v', 'c', 'z', 'b', 'u']
        s_win = {g: Stage(sem(f's_win_{g}'), 16) for g in GROUPS}
        s_wout = Stage(sem("s_wout"), 16)
        s_pj = Stage(sem("s_proj"), 20)
        s_pA = Stage(sem("s_projA"), 14)
        s_pV = Stage(sem("s_projV"), 6)
        s_kz = Stage(sem("s_kz"), 1)
        s_rope = Stage(sem("s_rope"), 2)
        s_qtp = Stage(sem("s_qtp"), 4)
        s_qtA = Stage(sem("s_qtA"), 4)
        s_qtV = Stage(sem("s_qtV"), 4)
        s_vn = Stage(sem("s_vn"), 4)
        s_gp = Stage(sem("s_gatep"), 2)
        s_gm = Stage(sem("s_gmlp"), 4)
        s_conv = Stage(sem("s_conv"), 1)
        s_nsink = Stage(sem("s_nsink"), 1)
        s_sc = Stage(sem("s_scores"), 32)
        s_nm = Stage(sem("s_max"), 32)
        s_ex = Stage(sem("s_exp"), 32)
        s_es = Stage(sem("s_expsink"), 4)
        s_pt = Stage(sem("s_probT"), 32)
        s_ptA = Stage(sem("s_probTA"), 16)
        s_ptV = Stage(sem("s_probTV"), 16)
        s_pv = Stage(sem("s_pv"), 32)
        s_on = Stage(sem("s_attn"), 4)
        s_ot = Stage(sem("s_attnT"), 4)
        s_om = Stage(sem("s_attn_mix"), 4)
        s_g1 = Stage(sem("s_g1"), 32)
        s_op = Stage(sem("s_outp"), 8)
        s_og = Stage(sem("s_outg"), 8)
        s_ox = Stage(sem("s_outx"), 8)
        s_a2 = Stage(sem("s_a2"), 80)
        s_ss2 = Stage(sem("s_ss2"), 4)
        s_h2 = Stage(sem("s_h2"), 4)
        s_h2p = Stage(sem("s_h2T"), 8)
        s_h2A = Stage(sem("s_h2TA"), 4)
        s_h2V = Stage(sem("s_h2TV"), 4)
        s_rc = Stage(sem("s_rconst"), 16)
        s_lq = Stage(sem("s_logit_quarters"), 4)
        s_lqc = Stage(sem("s_logit_quarters_copied"), 4)
        s_lg = Stage(sem("s_logits"), 4)
        s_sig = Stage(sem("s_sigmoid"), 1)
        s_msk = Stage(sem("s_mask"), 1)
        s_pre = Stage(sem("s_prefix"), 1)
        s_slot = Stage(sem("s_slot_numbers"), 1)
        s_pos = Stage(sem("s_pos"), 1)
        s_hz = sem('s_hsort_zero')
        s_scat = Stage(sem("s_scatter"), 128)
        s_we = [[sem(f"s_expert_{r}_{i}") for i in range(6)] for r in range(RING)]

        def weights_at(l, r, use):
            return (l * len(range(r, NE, RING)) + use) * 16

        s_hrow = lsem('s_hrow')
        s_hTp = lsem('s_hTp')
        s_hT = lsem('s_hT')
        s_gu = lsem('s_gateup')
        s_si = lsem('s_silu')
        s_a = lsem('s_a')
        s_at = lsem('s_aTp')
        s_aT = lsem('s_aT')
        s_d = lsem('s_down')
        s_y = lsem('s_y')
        s_yd = lsem('s_ystored')
        s_g2 = Stage(sem("s_g2"), 32)
        s_yg = [Stage(sem(f"s_ygather_{i}"), 64 if i == 0 else 32) for i in range(3)]
        s_yl = Stage(sem("s_ylow_scaled"), 4)
        s_comb = Stage(sem("s_combined"), 4)
        s_fg = sem('s_final_g')
        s_ssf = sem('s_ss_final')
        s_fin = sem('s_final')
        s_out = sem('s_out')
        s_r1, s_r2, s_vs, s_rv = (Stage(sem(n), 4) for n in ("s_root1", "s_root2", "s_vsum", "s_rootv"))
        s_rf = sem("s_root_final")
        s_yz = sem("s_ysort_rest")
        s_pl = sem("s_pool_chain")
        s_passed, s_pool_passed = sem("s_passed"), sem("s_pool_passed")
        s_dv = sem("s_dve_chain")
        s_ac = sem('s_act_chain')

        def proj_jobs(l):
            jobs = [("q", t, "A") for t in range(NT[l])]
            jobs += [("kv", t, "V") for t in range(NALL)]
            jobs += [("v", t, "A") for t in range(NT[l])]
            jobs += [("c", j, "A") for j in range(2)] + [("z", j, "V") for j in range(2)]
            jobs += [("b", j, "A") for j in range(2)] + [("u", j, "A") for j in range(2)]
            return jobs

        win_at = {"q": 0, "kv": W_C, "v": W_C + KV2, "c": W_C + KV2 + W_A, "z": W_C + KV2 + W_A + W_B,
                  "b": W_C + KV2 + W_A + 2 * W_B, "u": W_C + KV2 + W_A + 3 * W_B}

        MOD_JOBS = {0: 4, 1: 5, 2: 6, 3: 7, 5: 8, 7: 9, 9: 10, 11: 11, 12: 12, 13: 13, 14: 14, 15: 15,
                    16: 16, 17: 17, 18: 18, 19: 19}
        MOD_STEPS = {3: 20, 7: 21, 11: 22, 15: 23}

        def mod_bank(piece):
            return pb[(4 if piece < 10 else 2) + piece % 2]

        def evacuated(jobs, upto, eng):
            return sum(1 for j in jobs[:upto] if j[2] == eng)

        cols_of = {"q": (COL_Q, W_C), "kv": (COL_K, KV2), "v": (COL_V, W_A), "c": (COL_C, W_B),
                   "z": (COL_Z, W_B), "b": (COL_B, W_B), "u": (COL_U, W_A)}

        def steps(l):
            return [(t, h) for t in range(NT[l]) for h in range(NH)]

        def keys(t):
            return (0, 512) if t < NX else (256, 256)

        def pt_engine(i):
            return "A" if i % 2 == 0 else "V"

        def pt_count(i, eng):
            return i // 2 + 1 if eng == "A" else (i + 1) // 2

        MTC = {(part, s): s * 16 + n * 8 for s in range(2) for n, part in enumerate(["sh1", "sc1"])}
        MT_N1, MT_CONV = 32, 40
        N_ROWS = 46

        def mod_part(l, s, n):
            return mod_d[l, s, n * D:(n + 1) * D].partition_broadcast(P)

        block = es.enter_context(nc.Block())

        @block.sync
        def _(sp):
            def load_mod(m):
                l, n, kh = m // 12, m // 2 % 6, m % 2
                if m >= FIRST:
                    sp.wait_ge(s_modpe, m - 1 if m > FIRST + 1 else FIRST)
                window.room(2 * MB)
                window.started(2 * MB, s_wm[m % 4], 16 * (m // 4 + 1))
                sp.dma_start(wmodbuf(m), w_mod[l, kh * HK * P:(kh + 1) * HK * P, n * D:(n + 1) * D]
                             .rearrange("(k p) n -> p k n", p=P)).then_inc(s_wm[m % 4], 16)

            def load_win(l, g):
                c0, n = cols_of[g]
                window.room(n * 4 * D)
                window.started(n * 4 * D, s_win[g].sem, s_win[g].at(l, 16))
                sp.dma_start(win(l, g), w_in[l, :, c0:c0 + n].rearrange("(k p) n -> p k n", p=P)).then_inc(s_win[g].sem, 16)

            def load_wout(l):
                window.room(4 * MB)
                window.started(4 * MB, s_wout.sem, s_wout.at(l, 16))
                sp.dma_start(wout(l), w_out[l].rearrange("(k p) n -> p k n", p=P)).then_inc(s_wout.sem, 16)

            def load_small(l):
                sp.dma_start(ws_raw, w_s[l].rearrange("h p q -> p h q")).then_inc(s_small.sem, 16)
                for h in range(A_GROUPS):
                    r = 64 * (h % 2)
                    sp.dma_start(bsb[r:r + 64, h // 2, :], b_s[l, h].partition_broadcast(64)).then_inc(s_small.sem, 16)
                sp.dma_start(gvb[:, :], gmlp_g[l].partition_broadcast(P)).then_inc(s_small.sem, 16)
                sp.dma_start(sinkb[:, :], attn_sink[l].partition_broadcast(P)).then_inc(s_small.sem, 16)
                sp.wait_ge(s_modw, 32 * (6 * l + 2))
                sp.dma_start(rows[0:32, :], mod_d[l, :, 0:2 * D].rearrange("s (r p) -> s r p", p=P)).then_inc(s_row.sem, 16)
                sp.dma_start(rows[32:40, :], norm1_g[l].rearrange("(k p) -> k p", p=P)).then_inc(s_row.sem, 16)
                sp.dma_start(rows[40:46, :], conv_w[l].rearrange("w (j p) -> (w j) p", p=P)).then_inc(s_row.sem, 16)

            window = Window(sp, 4 * MB)

            def expert_parts(l, e, n):
                for w, d, k in ((w_gate, wgate(n), KD), (w_up, wup(n), KD), (w_down, wdown(n), KF)):
                    for hf in range(2):
                        rows_ = slice(hf * k // 2 * P, (hf + 1) * k // 2 * P)
                        src = (w[l, e, rows_, :].rearrange("(k p) n -> p k n", p=P) if isinstance(e, int)
                               else w[l, bass.ds(e, 1), rows_, :].rearrange("a (k p) n -> p (a k) n", p=P))
                        yield d[:, hf * k // 2:(hf + 1) * k // 2, :], src

            def load_expert(l, e, n):
                r = n % RING
                for i, (dst, src) in enumerate(expert_parts(l, e, n)):
                    window.room(MB)
                    sp.dma_start(dst, src).then_inc(s_we[r][i], 16)
                    window.started(MB, s_we[r][i], weights_at(l, r, e // RING + 1))

            def load_expert_looped(l, e, n, use):
                r, q = n % RING, (n - 1) % RING
                before = use if n > l else use - 1
                for i, (dst, src) in enumerate(expert_parts(l, e, n)):
                    if i < 3:
                        sp.wait_ge(s_we[q][i + 3], before * 16 + weights_at(l, q, 0))
                    else:
                        sp.wait_ge(s_we[r][i - 3], use * 16 + weights_at(l, r, 0))
                    sp.dma_start(dst, src).then_inc(s_we[r][i], 16)

            sp.dma_start(cst[:, :], consts).then_inc(s_const, 16)
            crow = work(0, 9216, 128)
            sp.dma_start(crow[0:KD, :], c.rearrange("a (k p) -> (a k) p", p=P)).then_inc(s_cvec, 16)
            sp.dma_start(crow[KD:2 * KD, :], c_ctx.rearrange("(k p) -> k p", p=P)).then_inc(s_cvec, 16)
            sp.dma_start(rwb[:, :, :], router_w.rearrange("(k p) n -> p k n", p=P)).then_inc(s_const, 16)
            sp.dma_start(rbb[:, :], router_b.partition_broadcast(P)).then_inc(s_const, 16)
            for m in range(FIRST):
                load_mod(m)
            for l in range(DEPTH):
                for s in range(2):
                    sp.dma_start(mod_d[l, s, :], b_mod[l, :]).then_inc(s_binit, 16)
            sp.dma_start(xres[:, 0:NX, :], x.rearrange("a (t p) d -> p (a t) d", p=P)).then_inc(s_x[0], 16)
            sp.dma_start(xres[:, NX:NALL, :], ctx.rearrange("a (t p) d -> p (a t) d", p=P)).then_inc(s_x[1], 16)
            load_win(0, "q")
            load_win(0, "kv")
            load_small(0)
            m = FIRST
            for g in GROUPS[2:]:
                load_win(0, g)
                for _ in range(3):
                    load_mod(m)
                    m += 1
            load_mod(m)
            for l in range(DEPTH):
                sp.wait_ge(s_pj.sem, s_pj.at(l, 2 * NT[l] + NALL + 4))
                load_expert(l, 0, l)
                if l == 0:
                    for m in range(20, 24):
                        load_mod(m)
                    sp.wait_ge(s_modpe, 24)
                    load_wout(0)
                sp.wait_ge(s_pj.sem, s_pj.at(l, len(proj_jobs(l))))
                sp.wait_ge(s_conv.sem, s_conv.at(l, 1))
                for s in range(NT[l] // 2):
                    dst = cz(l).rearrange("p j t -> p (j t)") if s == 0 else ybuf[:, :]
                    sp.dma_start(dst, mod_part(l, s, 2)).then_inc(s_g1.sem, 16)
                for s in range(NT[l] // 2):
                    sp.dma_start(work(l, 2048 * s, 1024), mod_part(l, s, 4)).then_inc(s_a2.sem, 16)
                    sp.dma_start(work(l, 2048 * s + 1024, 1024), mod_part(l, s, 3)).then_inc(s_a2.sem, 16)
                sp.wait_ge(s_gp.sem, s_gp.at(l, 2))
                sp.dma_start(vbuf[:, :], norm2_g[l].partition_broadcast(P)).then_inc(s_a2.sem, 16)
                sp.wait_ge(s_qtp.sem, s_qtp.at(l, NALL))
                sp.dma_start(work(l, 9216, 528), rconsts).then_inc(s_rc.sem, 16)
                sp.wait_ge(s_op.sem, s_op.at(l, 2 * NT[l]))
                load_expert(l, 1, l + 1)
                sp.wait_ge(s_h2.sem, s_h2.at(l, NT[l]))
                for s in range(NT[l] // 2):
                    sp.dma_start(vbuf[:, :] if s == 0 else ybuf[:, :], mod_part(l, s, 5)).then_inc(s_g2.sem, 16)
                sp.wait_ge(s_pos.sem, s_pos.at(l, 1))
                sp.wait_ge(s_scat.sem, s_scat.at(l, 32 * NT[l]))
                load_expert(l, 2, l + 2)
                if l + 1 < DEPTH:
                    load_small(l + 1)
                with sp.Fori(0, (NE - 1) // RING - 1) as i:
                    for j in range(RING):
                        first = sp.value_load(tab[l][0:1, bass.ds(i * RING + (j + 1), 1)], min_val=0, max_val=NTILE)
                        sp.wait_ge(s_d[l], first)
                        load_expert_looped(l, i * RING + (RING + j), l + j, i + 2)
                window.flying = []
                first = sp.value_load(tab[l][0:1, NE - 3:NE - 2], min_val=0, max_val=NTILE)
                sp.wait_ge(s_d[l], first)
                load_expert(l, NE - 1, NE - 1 + l)
                if l + 1 < DEPTH:
                    first = sp.value_load(tab[l][0:1, NE - 2:NE - 1], min_val=0, max_val=NTILE)
                    sp.wait_ge(s_d[l], first)
                    for g in GROUPS[:5]:
                        load_win(l + 1, g)
                    first = sp.value_load(tab[l][0:1, NE - 1:NE], min_val=0, max_val=NTILE)
                    sp.wait_ge(s_d[l], first)
                    for g in GROUPS[5:]:
                        load_win(l + 1, g)
                    sp.wait_ge(s_comb.sem, s_comb.at(l, NT[l]))
                    load_wout(l + 1)
                else:
                    sp.wait_ge(s_scat.sem, s_scat.at(l, 32 * NT[l]))
                    sp.dma_start(qtbuf[:, 0:D], final_g.partition_broadcast(P)).then_inc(s_fg, 16)
            for t in range(NX):
                sp.wait_ge(s_fin, t + 1)
                sp.dma_start(out[0, t * P:(t + 1) * P, :], hr(DEPTH - 1, t)).then_inc(s_out, 16)
            sp.wait_ge(s_out, 16 * NX)

        @block.gpsimd
        def _(pool):
            nc.gpsimd.memset(work(0, 9984, 256), 0.0).then_inc(s_sctz, 1)

            def store_mod(pieces):
                for n in pieces:
                    pool.wait_ge(s_mr, n + 1)
                    for s in range(2):
                        pool.dma_start(mod_d[n // 6, s, (n % 6) * D:(n % 6 + 1) * D].rearrange("(j n) -> j n", j=4),
                                       mrow[s:P:32, :], accum_op=ALU.add).then_inc(s_modw, 16)

            pl = Tally(pool, s_pl)

            def inv_root(dst, src, n):
                pl.link(nc.gpsimd.tensor_scalar(dst, src, 1.0 / n, EPS, ALU.mult, ALU.add))
                return nc.gpsimd.tensor_tensor(dst, dst, half, ALU.pow)

            half = st[:, 5, NALL:NALL + 1]
            pl.link(nc.gpsimd.memset(half, -0.5))

            pool.wait_ge(s_binit, 64)
            store_mod(range(2))
            for l in range(DEPTH):
                if l == 0:
                    nc.gpsimd.memset(qtbuf[:, 2048:4096], 0.0).then_inc(s_kz.sem, 1)
                for t in range(NALL):
                    pool.wait_ge(s_ss.sem, s_ss.at(l, t + 1))
                    inv_root(st[:, 1, t:t + 1], st[:, 0, t:t + 1], D).then_inc(s_r1.sem, 1)
                if l == 0:
                    store_mod(range(2, 4))
                for t in range(NT[l]):
                    pool.wait_ge(s_vs.sem, s_vs.at(l, t + 1))
                    inv_root(st[:, 5, t:t + 1], st[:, 4, t:t + 1], W_A).then_inc(s_rv.sem, 1)
                if l == 0:
                    store_mod(range(4, 10))
                    pool.wait_ge(s_pj.sem, s_pj.at(0, 20))
                    pool.wait_ge(s_kz.sem, s_kz.at(0, 1))
                    for n in range(NTILE):
                        pool.dma_start(hsort[n * SLOTS:(n + 1) * SLOTS, :], qtbuf[64:128, 2048:3072]).then_inc(s_hz, 16)
                    store_mod(range(10, 12))
                for t in range(NT[l]):
                    pool.wait_ge(s_ss2.sem, s_ss2.at(l, t + 1))
                    inv_root(st[:, 3, t:t + 1], st[:, 2, t:t + 1], D).then_inc(s_r2.sem, 1)
                if l == 0:
                    pool.wait_ge(s_hz, 16 * NTILE)
                pool.wait_ge(s_slot.sem, s_slot.at(l, 1))
                pool.sem_inc(s_pool_passed, 1)
                for t in range(NT[l]):
                    for k in range(2):
                        pool.indirect_dma_start(
                            out=hsort, out_offset=bass.IndirectOffsetOnAxis(ap=posi[:, k, t:t + 1].bitcast(U32), axis=0),
                            in_=h2[:, t, :], in_offset=None).then_inc(s_scat.sem, 16)
                pool.wait_ge(s_scat.sem, s_scat.at(l, 32 * NT[l]))
                pool.dma_start(hrow, hsort[0:SLOTS, :]).then_inc(s_hrow[l], 16)
                total = pool.value_load(tab[l][0:1, NE:NE + 1], min_val=NE, max_val=NTILE - 1)
                pool.wait_ge(s_hTp[l], 1)
                pool.dma_start(hrow, hsort[SLOTS:2 * SLOTS, :]).then_inc(s_hrow[l], 16)
                if l == 0:
                    lacking = pool.value_load(tab[l][0:1, NE + 1:NE + 2], min_val=1, max_val=NTILE - NE)
                    with pool.Fori(0, lacking) as i:
                        pool.dma_start(ysort[bass.ds((i * -1 + (NTILE - 1)) * SLOTS, SLOTS), :],
                                       hsort[bass.ds((i * -1 + (NTILE - 1)) * SLOTS, SLOTS), :]).then_inc(s_yz, 16)
                with pool.Fori(1, total) as T:
                    pool.wait_ge(s_hTp[l], T + 1)
                    pool.dma_start(hrow, hsort[bass.ds((T + 1) * SLOTS, SLOTS), :]).then_inc(s_hrow[l], 16)
                if l + 1 < DEPTH:
                    nc.gpsimd.memset(qtbuf[:, 2048:4096], 0.0).then_inc(s_kz.sem, 1)
                if l == 0:
                    pool.wait_ge(s_yz, lacking * 16)
                pool.wait_ge(s_hrow[l], total * 16 + 16)
                pool.wait_ge(s_yd[l], total * 32 + 32)
                pool.sem_inc(s_pool_passed, 1)
                for t in range(NT[l]):
                    if t >= 3:
                        pool.wait_ge(s_comb.sem, s_comb.at(l, t - 2))
                    for k in range(2):
                        pool.indirect_dma_start(
                            out=ybuf2(t, k), out_offset=None, in_=ysort,
                            in_offset=bass.IndirectOffsetOnAxis(ap=posi[:, k, t:t + 1].bitcast(U32), axis=0)).then_inc(s_yg[t % 3].sem, 16)
            for t in range(NX):
                pool.wait_ge(s_ssf, t + 1)
                inv_root(st[:, 1, t:t + 1], st[:, 0, t:t + 1], D).then_inc(s_rf, 1)

        @block.scalar
        def _(act):
            ac = Tally(act, s_ac)
            def copy_mod(piece):
                act.wait_ge(s_modpe, 2 * piece + 2)
                if piece:
                    act.wait_ge(s_modw, 32 * piece)
                nc.scalar.copy(mrow[:, :], mod_bank(piece)[:, 0:MQ]).then_inc(s_mr, 1)

            def scale_low(l, t):
                act.wait_ge(s_yg[t % 3].sem, s_yg[t % 3].at(l, 32 * (t // 3 + 1)))
                nc.scalar.activation(ybuf2(t, 0), ybuf2(t, 0), ACT.Copy, scale=wtk[:, 0, t:t + 1]).then_inc(s_yl.sem, 1)

            act.wait_ge(s_sctz, 1)
            act.wait_ge(s_ctp, 1)
            nc.scalar.activation(sct[:, :, 0:2], pb[0][:, 0:16].rearrange("p (s k) -> p k s", s=2), ACT.Silu).then_inc(s_sct, 1)
            copy_mod(0)
            copy_mod(1)
            for l in range(DEPTH):
                for t in range(NALL):
                    if l > 0:
                        if t == 1:
                            scale_low(l - 1, 2)
                        act.wait_ge(s_comb.sem, s_comb.at(l - 1, t + 1))
                    elif t in (0, NX):
                        act.wait_ge(s_x[t // NX], 16)
                    if t >= 2:
                        act.wait_ge(s_ta.sem, s_ta.at(l, 2 * (t - 1)))
                    nc.scalar.activation(hr(l, t % 2), xres[:, t, :], ACT.Square, accum_out=st[:, 0, t:t + 1]).then_inc(s_ss.sem, 1)
                    if t == 1:
                        if l > 0:
                            scale_low(l - 1, 3)
                        act.wait_ge(s_mt.sem, s_mt.at(l, 1))
                    if t >= 1:
                        norm1_evac(nc, act, l, t - 1, s_ta, s_tA, pb, ht(l), a1t, mt, MTC, NX)
                norm1_evac(nc, act, l, NALL - 1, s_ta, s_tA, pb, ht(l), a1t, mt, MTC, NX)
                for n, (kind, i, eng) in enumerate(proj_jobs(l)):
                    if l == 0 and MOD_JOBS.get(n - 1, 0) % 2 == 1:
                        copy_mod(MOD_JOBS[n - 1] // 2)
                    if eng != "A":
                        continue
                    act.wait_ge(s_pj.sem, s_pj.at(l, n + 1))
                    bank = pb[n % 4]
                    N = NT[l] * P
                    if kind == "q":
                        ins = nc.scalar.copy(qk[:, i, 0:W_C], bank[:, :])
                    elif kind == "v":
                        ins = nc.scalar.activation(vt[:, i, :], bank[:, 0:W_A], ACT.Gelu_apprx_tanh)
                    elif kind == "c":
                        ins = nc.scalar.copy(cz(l)[:, i, 0:N], bank[:, 0:N])
                    elif kind == "b":
                        ins = nc.scalar.copy(mixt(l)[:, 2 + i, 0:N], bank[:, 0:N])
                    else:
                        ins = nc.scalar.activation(mixt(l)[:, i, 0:N], bank[:, 0:N], ACT.Gelu_apprx_tanh)
                    ins.then_inc(s_pA.sem, 1)
                if l == 0:
                    copy_mod(9)
                for t in range(NT[l]):
                    act.wait_ge(s_qtp.sem, s_qtp.at(l, t + 1))
                    nc.scalar.copy(qT[:, :, t * P:(t + 1) * P], pb[4 + 2 * (t % 2)][:, :].rearrange("p (b t) -> p b t", b=4)).then_inc(s_qtA.sem, 1)
                S = steps(l)

                def copy_pt(i):
                    if i >= 0 and pt_engine(i) == "A":
                        n = keys(S[i][0])[1]
                        act.wait_ge(s_pt.sem, s_pt.at(l, i + 1))
                        if i >= 2:
                            act.wait_ge(s_pv.sem, s_pv.at(l, i - 1))
                        nc.scalar.copy(probt(l, i % 2)[:, 0:n // P, :], pb[6 + i % 2][:, 0:n].rearrange("p (k q) -> p k q", q=P)).then_inc(s_ptA.sem, 1)

                def sink_prob(t):
                    act.wait_ge(s_esum.sem, s_esum.at(l, t + 1))
                    nc.scalar.activation(esink[:, :], esum[:, :], ACT.Exp).then_inc(s_es.sem, 1)

                for i, (t, h) in enumerate(S):
                    n = keys(t)[1]
                    act.wait_ge(s_nm.sem, s_nm.at(l, i + 1))
                    if i >= 2:
                        act.wait_ge(s_pt.sem, s_pt.at(l, i - 1))
                    if l == 0 and MOD_STEPS.get(i - 1, 0) % 2 == 1:
                        copy_mod(MOD_STEPS[i - 1] // 2)
                    if h == 1 and t >= 1:
                        sink_prob(t - 1)
                    if t >= 2 and h == 0:
                        act.wait_ge(s_on.sem, s_on.at(l, t - 1))
                    nc.scalar.activation(prob(l, i % 2)[:, 0:n], pb[4 + i % 2][:, 0:n], ACT.Exp, bias=nmx[:, t % 2, h:h + 1],
                                         scale=SCALE, accum_out=rsum[:, t % 2, h:h + 1]).then_inc(s_ex.sem, 1)
                    copy_pt(i - 1)
                copy_pt(len(S) - 1)
                sink_prob(NT[l] - 1)
                for t in range(NT[l]):
                    act.wait_ge(s_ot.sem, s_ot.at(l, t + 1))
                    nc.scalar.copy(mixt(l)[:, 4:8, t * P:(t + 1) * P], pb[2 + t % 2][:, :].rearrange("p (k q) -> p k q", k=4)).then_inc(s_om.sem, 1)
                def quarters(t):
                    act.wait_ge(s_lq.sem, s_lq.at(l, t + 1))
                    if t >= 1:
                        act.wait_ge(s_lg.sem, s_lg.at(l, t))
                    nc.scalar.copy(logit_quarters(l), pb[0][:, 0:P]).then_inc(s_lqc.sem, 1)

                for t in range(NT[l]):
                    act.wait_ge(s_ox.sem, s_ox.at(l, 2 * t + 2))
                    nc.scalar.activation(h2[:, t, :], xres[:, t, :], ACT.Square, accum_out=st[:, 2, t:t + 1]).then_inc(s_ss2.sem, 1)
                    if t >= 1:
                        quarters(t - 1)
                    act.wait_ge(s_h2p.sem, s_h2p.at(l, 2 * t + 1))
                    if t >= 2:
                        act.wait_ge(s_lq.sem, s_lq.at(l, t - 1))
                    nc.scalar.copy(hr(l, t % 2)[:, 0:512], pb[4 + 2 * (t % 2)][:, :]).then_inc(s_h2A.sem, 1)
                quarters(NT[l] - 1)
                act.wait_ge(s_lg.sem, s_lg.at(l, NT[l]))
                nc.scalar.activation(work(l, rt0, 16 * NT[l]), pb[1][:, 0:16 * NT[l]], ACT.Sigmoid).then_inc(s_sig.sem, 1)
                act.wait_ge(s_pos.sem, s_pos.at(l, 1))
                total = act.value_load(tab[l][0:1, NE:NE + 1], min_val=NE, max_val=NTILE - 1)
                act.sem_inc(s_y[l], 1)
                act.sem_inc(s_yd[l], 32)
                with act.Fori(0, total) as T:
                    for hf in range(2):
                        act.wait_ge(s_gu[l], T * 2 + (hf + 1))
                        nc.scalar.activation(sg[:, hf * 256:(hf + 1) * 256], pb[hf][0:SLOTS, 0:256], ACT.Silu).then_inc(s_si[l], 1)
                    act.wait_ge(s_d[l], T + 1)
                    act.wait_ge(s_yd[l], T * 32 + 32)
                    nc.scalar.copy(ysb, pb[4][:, :]).then_inc(s_y[l], 1)
                    act.wait_ge(s_y[l], T + 2)
                    for hf in range(2):
                        act.dma_start(ysort[bass.ds(T * SLOTS, SLOTS), hf * 512:(hf + 1) * 512],
                                      ysb[hf * SLOTS:(hf + 1) * SLOTS, :]).then_inc(s_yd[l], 16)
                for t in range(2):
                    scale_low(l, t)
            l = DEPTH - 1
            for t in range(NX):
                act.wait_ge(s_comb.sem, s_comb.at(l, t + 1))
                nc.scalar.activation(hr(l, t), xres[:, t, :], ACT.Square, accum_out=st[:, 0, t:t + 1]).then_inc(s_ssf, 1)

        @block.tensor
        def _(pe):
            pe.wait_ge(s_const, 48)
            pe.wait_ge(s_cvec, 32)
            pe.transpose(pb[0][:, 0:16], work(0, 9216, 128)[0:16, :], ident[0:16, 0:16]).then_inc(s_ctp, 1)
            pe.wait_ge(s_sct, 1)

            def modulate(m):
                piece, kh = m // 2, m % 2
                pe.wait_ge(s_wm[m % 4], 16 * (m // 4 + 1))
                if kh == 0 and piece >= 2:
                    pe.wait_ge(s_mr, piece - 1)
                for k in range(HK):
                    for j in range(4):
                        mm = pe.matmul(mod_bank(piece)[32 * j:32 * j + 32, 0:MQ], sct[:, kh * HK + k, :],
                                       wmodbuf(m)[:, k, j * MQ:(j + 1) * MQ],
                                       start=(kh == 0 and k == 0), stop=(kh == 1 and k == HK - 1), tile_position=(0, 32 * j))
                mm.then_inc(s_modpe, 1)

            for m in range(FIRST):
                modulate(m)
            for l in range(DEPTH):
                J = proj_jobs(l)
                pe.wait_ge(s_row.sem, s_row.at(l, 48))
                pe.transpose(pb[2][:, 0:N_ROWS], rows[0:N_ROWS, :], ident[0:N_ROWS, 0:N_ROWS]).then_inc(s_mtp.sem, 1)
                pe.wait_ge(s_small.sem, s_small.at(l, 16 * 7))
                for h in range(A_GROUPS):
                    mm = pe.transpose(pb[3][:, h * P:(h + 1) * P], ws_raw[:, h, :], ident)
                mm.then_inc(s_wsp.sem, 1)
                pe.wait_ge(s_mr, 2)
                for t in range(NALL):
                    pe.wait_ge(s_hr.sem, s_hr.at(l, t + 1))
                    for hf in range(2):
                        if t >= 2:
                            copied = s_tA if hf == 0 else s_tV
                            pe.wait_ge(copied.sem, copied.at(l, t - 1))
                        for k in range(4):
                            kk = 4 * hf + k
                            mm = pe.transpose(pb[4 + (2 * t + hf) % 4][:, k * P:(k + 1) * P], hr(l, t % 2)[:, kk * P:(kk + 1) * P], ident)
                        mm.then_inc(s_ta.sem, 1)
                pe.wait_ge(s_tA.sem, s_tA.at(l, NALL))
                pe.wait_ge(s_tV.sem, s_tV.at(l, NALL))
                pe.wait_ge(s_mt.sem, s_mt.at(l, 1))
                pe.wait_ge(s_wst.sem, s_wst.at(l, 1))
                for n, (kind, i, _) in enumerate(J):
                    bank = pb[n % 4]
                    pe.wait_ge(s_win[kind].sem, s_win[kind].at(l, 16))
                    if n >= 4:
                        if J[n - 4][2] == "A":
                            pe.wait_ge(s_pA.sem, s_pA.at(l, evacuated(J, n - 3, "A")))
                        else:
                            pe.wait_ge(s_pV.sem, s_pV.at(l, evacuated(J, n - 3, "V")))
                    N = cols_of[kind][1]
                    for k in range(KD):
                        if kind in ("q", "kv", "v"):
                            mm = pe.matmul(bank[:, 0:N], ht(l)[:, k, i * P:(i + 1) * P], win(l, kind)[:, k, :],
                                           start=(k == 0), stop=(k == KD - 1))
                        else:
                            mm = pe.matmul(bank[:, 0:NT[l] * P], win(l, kind)[:, k, i * P:(i + 1) * P],
                                           ht(l)[:, k, 0:NT[l] * P], start=(k == 0), stop=(k == KD - 1))
                    mm.then_inc(s_pj.sem, 1)
                    if l == 0 and n in MOD_JOBS:
                        modulate(MOD_JOBS[n])
                if l == 0:
                    pe.wait_ge(s_mr, 10)
                for t in range(NALL):
                    if t < NX:
                        pe.wait_ge(s_rope.sem, s_rope.at(l, t + 1))
                    else:
                        pe.wait_ge(s_pV.sem, s_pV.at(l, NALL))
                        pe.wait_ge(s_pA.sem, s_pA.at(l, min(t + 1, NT[l])))
                    if t >= 2:
                        pe.wait_ge(s_qtA.sem, s_qtA.at(l, min(t - 1, NT[l])))
                        pe.wait_ge(s_qtV.sem, s_qtV.at(l, t - 1))
                    if t < NT[l]:
                        for b in range(4):
                            pe.transpose(pb[4 + 2 * (t % 2)][:, b * P:(b + 1) * P], qk[:, t, b * P:(b + 1) * P], ident)
                    for b in range(2):
                        mm = pe.transpose(pb[5 + 2 * (t % 2)][:, b * P:(b + 1) * P], qk[:, t, W_C + b * P:W_C + (b + 1) * P], ident)
                    mm.then_inc(s_qtp.sem, 1)
                pe.wait_ge(s_vn.sem, s_vn.at(l, NT[l]))
                pe.wait_ge(s_pA.sem, s_pA.at(l, evacuated(J, len(J), "A")))
                pe.wait_ge(s_pV.sem, s_pV.at(l, evacuated(J, len(J), "V")))
                for j in range(2):
                    for t in range(NT[l]):
                        for r in range(2):
                            h = 2 * j + r
                            mm = pe.matmul(pb[j][64 * r:64 * r + 64, t * P:(t + 1) * P], vt[:, t, h * 64:(h + 1) * 64], wst[:, h, :],
                                           start=True, stop=True, tile_position=(0, 64 * r))
                    mm.then_inc(s_gp.sem, 1)
                pe.wait_ge(s_qtA.sem, s_qtA.at(l, NT[l]))
                pe.wait_ge(s_qtV.sem, s_qtV.at(l, NALL))
                pe.wait_ge(s_gm.sem, s_gm.at(l, 3))
                S = steps(l)

                def score(i):
                    t, h = S[i]
                    k0, n = keys(t)
                    if i >= 2:
                        pe.wait_ge(s_ex.sem, s_ex.at(l, i - 1))
                    pe.matmul(pb[4 + i % 2][:, 0:n], qT[:, h // 2, t * P:(t + 1) * P], kz[:, h % 2, h // 4, k0:k0 + n],
                              start=True, stop=True).then_inc(s_sc.sem, 1)

                def turn(i):
                    t, h = S[i]
                    n = keys(t)[1]
                    pe.wait_ge(s_ex.sem, s_ex.at(l, i + 1))
                    if i >= 2:
                        e = pt_engine(i - 2)
                        copied = s_ptA if e == "A" else s_ptV
                        pe.wait_ge(copied.sem, copied.at(l, pt_count(i - 2, e)))
                    for k in range(n // P):
                        mm = pe.transpose(pb[6 + i % 2][:, k * P:(k + 1) * P], prob(l, i % 2)[:, k * P:(k + 1) * P], ident)
                    mm.then_inc(s_pt.sem, 1)

                def values(i):
                    t, h = S[i]
                    k0, n = keys(t)
                    e = pt_engine(i)
                    copied = s_ptA if e == "A" else s_ptV
                    pe.wait_ge(copied.sem, copied.at(l, pt_count(i, e)))
                    if h == 0 and t >= 2:
                        pe.wait_ge(s_on.sem, s_on.at(l, t - 1))
                    v0 = (h // 4) * HD
                    for k in range(n // P):
                        mm = pe.matmul(pb[t % 2][:, h * HD:(h + 1) * HD], probt(l, i % 2)[:, k, :], vv[:, k0 // P + k, v0:v0 + HD],
                                       start=(k == 0), stop=(k == n // P - 1))
                    mm.then_inc(s_pv.sem, 1)

                def turn_out(t):
                    pe.wait_ge(s_on.sem, s_on.at(l, t + 1))
                    if t >= 2:
                        pe.wait_ge(s_om.sem, s_om.at(l, t - 1))
                    for b in range(4):
                        mm = pe.transpose(pb[2 + t % 2][:, b * P:(b + 1) * P], qk[:, t, b * P:(b + 1) * P], ident)
                    mm.then_inc(s_ot.sem, 1)

                score(0)
                for i in range(len(S)):
                    if i + 1 < len(S):
                        score(i + 1)
                    turn(i)
                    if i >= 1:
                        values(i - 1)
                    if l == 0 and i in MOD_STEPS:
                        modulate(MOD_STEPS[i])
                values(len(S) - 1)
                if l == 0:
                    pe.wait_ge(s_mr, NP)
                for t in range(NT[l]):
                    turn_out(t)
                pe.wait_ge(s_wout.sem, s_wout.at(l, 16))
                pe.wait_ge(s_om.sem, s_om.at(l, NT[l]))
                pe.wait_ge(s_gm.sem, s_gm.at(l, 4))
                pe.wait_ge(s_conv.sem, s_conv.at(l, 1))
                def out_job(n):
                    t, hf = n // 2, n % 2
                    if n >= 2:
                        pe.wait_ge(s_og.sem, s_og.at(l, n - 1))
                    for k in range(KD):
                        mm = pe.matmul(pb[2 + n % 2][:, :], mixt(l)[:, k, t * P:(t + 1) * P], wout(l)[:, k, hf * 512:(hf + 1) * 512],
                                       start=(k == 0), stop=(k == KD - 1))
                    mm.then_inc(s_op.sem, 1)

                def turn_h2(t):
                    pe.wait_ge(s_h2.sem, s_h2.at(l, t + 1))
                    for hf in range(2):
                        if t >= 2:
                            copied = s_h2A if hf == 0 else s_h2V
                            pe.wait_ge(copied.sem, copied.at(l, t - 1))
                        for k in range(4):
                            kk = 4 * hf + k
                            mm = pe.transpose(pb[4 + 2 * (t % 2) + hf][:, k * P:(k + 1) * P], h2[:, t, kk * P:(kk + 1) * P], ident)
                        mm.then_inc(s_h2p.sem, 1)

                def logits(t):
                    pe.wait_ge(s_h2A.sem, s_h2A.at(l, t + 1))
                    pe.wait_ge(s_h2V.sem, s_h2V.at(l, t + 1))
                    if t >= 1:
                        pe.wait_ge(s_lqc.sem, s_lqc.at(l, t))
                    for k in range(KD):
                        j = k % 4
                        mm = pe.matmul(pb[0][32 * j:32 * j + NE, 0:P], rwb[:, k, :], hr(l, t % 2)[:, k * P:(k + 1) * P],
                                       start=(k < 4), stop=(k >= 4), tile_position=(0, 32 * j))
                    mm.then_inc(s_lq.sem, 1)

                def fold(t):
                    pe.wait_ge(s_lqc.sem, s_lqc.at(l, t + 1))
                    pe.matmul(pb[1][:, t * NE:(t + 1) * NE], logit_quarters(l), cst[:, C_FOLD:C_FOLD + NE],
                              start=True, stop=True).then_inc(s_lg.sem, 1)

                for n in range(2 * NT[l]):
                    out_job(n)
                    if n >= 4 and n % 2 == 0:
                        fold(n // 2 - 2)
                    if n >= 2 and n % 2 == 0:
                        turn_h2(n // 2 - 1)
                    if n >= 3 and n % 2 == 1:
                        logits((n - 3) // 2)
                fold(NT[l] - 2)
                turn_h2(NT[l] - 1)
                logits(NT[l] - 1)
                fold(NT[l] - 1)
                pe.wait_ge(s_msk.sem, s_msk.at(l, 1))
                pe.wait_ge(s_rc.sem, s_rc.at(l, 16))
                rc = work(l, 9216, 528)
                W = (NT[l] + 1) * NE
                pe.matmul(pb[1][:, 0:W], rc[:, R_BEFORE:R_BEFORE + P], chosen_experts(l)[:, 0:W], start=True, stop=False)
                for u in range(1, NT[l] + 1):
                    mm = pe.matmul(pb[1][:, u * NE:W], rc[:, R_ONES:R_ONES + P], chosen_experts(l)[:, 0:W - u * NE],
                                   start=False, stop=(u == NT[l]))
                mm.then_inc(s_pre.sem, 1)

                def turn_rows():
                    for k in range(KD):
                        mm = pe.transpose(pb[5][:, k * SLOTS:(k + 1) * SLOTS], hrow[:, k * P:(k + 1) * P], ident[0:SLOTS, 0:SLOTS])
                    mm.then_inc(s_hTp[l], 1)

                def tile(T, n):
                    pe.wait_ge(s_hT[l], T + 1)

                    def gate_up(hf, ks):
                        for k in ks:
                            for r, w in ((0, wgate(n)), (1, wup(n))):
                                mm = pe.matmul(pb[hf][64 * r:64 * r + 64, 0:256], hTe[:, k, :], w[:, k, hf * 256:(hf + 1) * 256],
                                               start=(k == 0), stop=(k == KD - 1), tile_position=(0, 64 * r))
                        if k == KD - 1:
                            mm.then_inc(s_gu[l], 1)

                    def turn_a(hf):
                        pe.wait_ge(s_a[l], T * 2 + (hf + 1))
                        pe.sem_inc(s_passed, 1)
                        for k in range(2):
                            mm = pe.transpose(pb[2 + hf][:, k * SLOTS:(k + 1) * SLOTS], ae[:, (2 * hf + k) * P:(2 * hf + k + 1) * P],
                                              ident[0:SLOTS, 0:SLOTS])
                        mm.then_inc(s_at[l], 1)

                    def down(hf):
                        pe.wait_ge(s_aT[l], T * 2 + (hf + 1))
                        for k in (2 * hf, 2 * hf + 1):
                            for r in range(2):
                                mm = pe.matmul(pb[4][64 * r:64 * r + 64, :], aTe[:, k, :], wdown(n)[:, k, r * 512:(r + 1) * 512],
                                               start=(k == 0), stop=(k == KF - 1), tile_position=(0, 64 * r))
                        return mm

                    gate_up(0, range(KD))
                    gate_up(1, range(KD // 2))
                    turn_a(0)
                    gate_up(1, range(KD // 2, KD))
                    pe.wait_ge(s_y[l], T + 1)
                    down(0)
                    turn_a(1)
                    pe.wait_ge(s_hrow[l], T * 16 + 32)
                    pe.sem_inc(s_passed, 1)
                    turn_rows()
                    mm = down(1)
                    mm.then_inc(s_d[l], 1)

                def expert(e, use, n):
                    r = n % RING
                    lo = pe.value_load(tab[l][0:1, bass.ds(e, 1)], min_val=0, max_val=NTILE)
                    hi = pe.value_load(tab[l][0:1, bass.ds(e + 1, 1)], min_val=0, max_val=NTILE)
                    for i in range(6):
                        pe.wait_ge(s_we[r][i], use * 16 + weights_at(l, r, 0))
                    pe.sem_inc(s_passed, 1)
                    with pe.Fori(lo, hi) as T:
                        tile(T, n)

                pe.wait_ge(s_hrow[l], 16)
                pe.wait_ge(s_pos.sem, s_pos.at(l, 1))
                turn_rows()
                with pe.Fori(0, (NE - 1) // RING) as i:
                    for j in range(RING):
                        expert(i * RING + j, i + 1, l + j)
                expert(NE - 1, (NE - 1) // RING + 1, NE - 1 + l)

        @block.vector
        def _(dve):
            dv = Tally(dve, s_dv)
            link = dv.link
            V = nc.vector

            def rows1(l, t):
                dve.wait_ge(s_r1.sem, s_r1.at(l, t + 1))
                V.tensor_scalar(hr(l, t % 2), xres[:, t, :], st[:, 1, t:t + 1], None, ALU.mult).then_inc(s_hr.sem, 1)

            for l in range(DEPTH):
                J = proj_jobs(l)
                N = NT[l] * P
                dve.wait_ge(s_mtp.sem, s_mtp.at(l, 1))
                link(V.tensor_copy(mt[:, 0:N_ROWS], pb[2][:, 0:N_ROWS]))
                for s in range(2):
                    c0 = MTC["sc1", s]
                    ins = V.scalar_tensor_tensor(out=a1t[:, s, :], in0=mt[:, c0:c0 + KD], scalar=1.0, in1=mt[:, MT_N1:MT_N1 + KD],
                                                 op0=ALU.add, op1=ALU.mult)
                ins.then_inc(s_mt.sem, 1)
                dve.wait_ge(s_mt.sem, s_mt.at(l, 1))
                dve.wait_ge(s_wsp.sem, s_wsp.at(l, 1))
                V.tensor_copy(wst[:, :, :], pb[3][:, :].rearrange("p (h q) -> p h q", h=A_GROUPS)).then_inc(s_wst.sem, 1)
                V.tensor_scalar(nsink[:, :], sinkb[:, :], -1.0, None, ALU.mult).then_inc(s_nsink.sem, 1)

                if l == 0:
                    rows1(l, 0)
                for t in range(NALL):
                    if t + 1 < NALL and (l == 0 or t + 1 >= 2):
                        if t + 1 >= 2:
                            dve.wait_ge(s_ta.sem, s_ta.at(l, 2 * t))
                        rows1(l, t + 1)
                    dve.wait_ge(s_ta.sem, s_ta.at(l, 2 * t + 2))
                    s = t // NX
                    for k in range(4):
                        kk = 4 + k
                        b0 = MTC["sh1", s] + kk
                        ins = V.tensor_scalar(ht(l)[:, kk, t * P:(t + 1) * P], pb[4 + (2 * t + 1) % 4][:, k * P:(k + 1) * P],
                                              a1t[:, s, kk:kk + 1], mt[:, b0:b0 + 1], ALU.mult, ALU.add)
                    ins.then_inc(s_tV.sem, 1)

                def rope(t):
                    if t < NX:
                        q3 = qk[:, t, :].rearrange("p (h a b c) -> p h a b c", a=2, b=2, c=16)
                        r3 = ropet(l).rearrange("p (h a b c) -> p h a b c", a=2, b=2, c=16)
                        sn = cst[:, C_SIN + t * HD:C_SIN + (t + 1) * HD].rearrange("p (a b c) -> p a b c", a=2, b=2)
                        cs = cst[:, C_COS + t * HD:C_COS + (t + 1) * HD]
                        nh = QW // HD
                        for a in range(2):
                            for b in range(2):
                                ins = V.tensor_tensor(r3[:, :, a, b, :], q3[:, :, a, 1 - b, :],
                                                      sn[:, a, b, :].unsqueeze(1).broadcast_to([P, nh, 16]), ALU.mult)
                        link(ins)
                        qf = qk[:, t, :].rearrange("p (h d) -> p h d", d=HD)
                        link(V.tensor_tensor(qf, qf, cs.unsqueeze(1).broadcast_to([P, nh, HD]), ALU.mult))
                        V.tensor_tensor(qk[:, t, :], qk[:, t, :], ropet(l), ALU.add).then_inc(s_rope.sem, 1)
                        dve.wait_ge(s_rope.sem, s_rope.at(l, t + 1))

                def norm_v(t):
                    link(V.tensor_tensor(yc_flat[:, 0:W_A], vt[:, t, :], vt[:, t, :], ALU.mult))
                    V.tensor_reduce(st[:, 4, t:t + 1], yc_flat[:, 0:W_A], AX, ALU.add).then_inc(s_vs.sem, 1)
                    dve.wait_ge(s_rv.sem, s_rv.at(l, t + 1))
                    V.scalar_tensor_tensor(out=vt[:, t, :], in0=vt[:, t, :], scalar=st[:, 5, t:t + 1], in1=gvb[:, :],
                                           op0=ALU.mult, op1=ALU.mult).then_inc(s_vn.sem, 1)
                    dve.wait_ge(s_vn.sem, s_vn.at(l, t + 1))

                yc_flat = ybuf[:, :]
                kvs = [n for n, j in enumerate(J) if j[0] == "kv"]
                zs = [n for n, j in enumerate(J) if j[0] == "z"]
                for t, n in enumerate(kvs):
                    dve.wait_ge(s_pj.sem, s_pj.at(l, n + 1))
                    kd = qk[:, t, W_C:W_C + 256].rearrange("p (v r d) -> p v r d", v=NKV, r=2)
                    src = pb[n % 4][:, 0:P].rearrange("p (v d) -> p v d", v=NKV).unsqueeze(2).broadcast_to([P, NKV, 2, HD])
                    V.tensor_copy(kd, src)
                    V.tensor_copy(vv[:, t, :], pb[n % 4][:, P:2 * P]).then_inc(s_pV.sem, 1)
                dve.wait_ge(s_pV.sem, s_pV.at(l, NALL))
                for t in range(NALL):
                    if t < NT[l]:
                        dve.wait_ge(s_pA.sem, s_pA.at(l, t + 1))
                    rope(t)
                for t in range(NT[l]):
                    dve.wait_ge(s_pA.sem, s_pA.at(l, NT[l] + t + 1))
                    norm_v(t)
                for j, n in enumerate(zs):
                    dve.wait_ge(s_pj.sem, s_pj.at(l, n + 1))
                    dve.wait_ge(s_pA.sem, s_pA.at(l, 2 * NT[l] + j + 1))
                    V.tensor_tensor(cz(l)[:, j, 0:N], pb[n % 4][:, 0:N], cz(l)[:, j, 0:N], ALU.mult).then_inc(s_pV.sem, 1)
                dve.wait_ge(s_pV.sem, s_pV.at(l, NALL + 2))
                for t in range(NALL):
                    dve.wait_ge(s_qtp.sem, s_qtp.at(l, t + 1))
                    if t == 0:
                        dve.wait_ge(s_kz.sem, s_kz.at(l, 1))
                    src = pb[5 + 2 * (t % 2)][:, 0:256].rearrange("p (v t) -> p v t", v=NKV)
                    V.tensor_copy(kz[0:64, 0, :, t * P:(t + 1) * P], src[0:64])
                    V.tensor_copy(kz[64:128, 1, :, t * P:(t + 1) * P], src[64:128]).then_inc(s_qtV.sem, 1)
                for j in range(2):
                    dve.wait_ge(s_gp.sem, s_gp.at(l, j + 1))
                    dve.wait_ge(s_pA.sem, s_pA.at(l, evacuated(J, len(J), "A")))
                    tmp = work(l, 0, 512)
                    g3 = tmp[:, 0:N].rearrange("p (t q) -> p t q", q=P)
                    V.tensor_tensor(g3, pb[j][:, 0:N].rearrange("p (t q) -> p t q", q=P),
                                    bsb[:, j, :].unsqueeze(1).broadcast_to([P, NT[l], P]), ALU.add).then_inc(s_gm.sem, 1)
                    dve.wait_ge(s_gm.sem, s_gm.at(l, 2 * j + 1))
                    V.tensor_tensor(mixt(l)[:, j, 0:N], mixt(l)[:, j, 0:N], tmp[:, 0:N], ALU.mult).then_inc(s_gm.sem, 1)
                    dve.wait_ge(s_gm.sem, s_gm.at(l, 2 * j + 2))
                for j in range(2):
                    w = [mt[:, MT_CONV + 2 * i + j:MT_CONV + 2 * i + j + 1] for i in range(3)]
                    zj = cz(l)[:, j, 0:N].rearrange("p (s t) -> p s t", t=256)
                    yj = yc[:, j, 0:N].rearrange("p (s t) -> p s t", t=256)
                    link(V.tensor_scalar(yj, zj, w[1], None, ALU.mult))
                    link(V.scalar_tensor_tensor(out=yj[:, :, 1:256], in0=zj[:, :, 0:255], scalar=w[0], in1=yj[:, :, 1:256],
                                                op0=ALU.mult, op1=ALU.add))
                    link(V.scalar_tensor_tensor(out=yj[:, :, 0:255], in0=zj[:, :, 1:256], scalar=w[2], in1=yj[:, :, 0:255],
                                                op0=ALU.mult, op1=ALU.add))
                    ins = V.tensor_tensor(mixt(l)[:, 2 + j, 0:N], mixt(l)[:, 2 + j, 0:N], yc[:, j, 0:N], ALU.mult)
                ins.then_inc(s_conv.sem, 1)
                S = steps(l)
                dve.wait_ge(s_nsink.sem, s_nsink.at(l, 1))

                def copy_pt(i):
                    if i >= 0 and pt_engine(i) == "V":
                        n = keys(S[i][0])[1]
                        dve.wait_ge(s_pt.sem, s_pt.at(l, i + 1))
                        if i >= 2:
                            dve.wait_ge(s_pv.sem, s_pv.at(l, i - 1))
                        V.tensor_copy(probt(l, i % 2)[:, 0:n // P, :], pb[6 + i % 2][:, 0:n].rearrange("p (k q) -> p k q", q=P)).then_inc(s_ptV.sem, 1)

                def normalise(t):
                    dve.wait_ge(s_pv.sem, s_pv.at(l, NH * (t + 1)))
                    dve.wait_ge(s_ex.sem, s_ex.at(l, NH * (t + 1)))
                    dve.wait_ge(s_es.sem, s_es.at(l, t + 1))
                    link(V.tensor_tensor(rden[:, :], rsum[:, t % 2, :], esink[:, :], ALU.add))
                    link(V.reciprocal(rden[:, :], rden[:, :]))
                    o3 = qk[:, t, 0:W_C].rearrange("p (h d) -> p h d", h=NH)
                    V.tensor_tensor(o3, pb[t % 2][:, :].rearrange("p (h d) -> p h d", h=NH),
                                    rden[:, :].unsqueeze(2).broadcast_to([P, NH, HD]), ALU.mult).then_inc(s_on.sem, 1)
                    dve.wait_ge(s_on.sem, s_on.at(l, t + 1))

                for i, (t, h) in enumerate(S):
                    n = keys(t)[1]
                    bank = pb[4 + i % 2]
                    dve.wait_ge(s_sc.sem, s_sc.at(l, i + 1))
                    if t < NX:
                        m0 = P if t == 0 else 0
                        link(V.tensor_tensor(bank[:, m0:m0 + P], bank[:, m0:m0 + P], cst[:, C_MASK + t * P:C_MASK + (t + 1) * P], ALU.add))
                    link(V.tensor_reduce(mx[:, h:h + 1], bank[:, 0:n], AX, ALU.max))
                    V.tensor_scalar(nmx[:, t % 2, h:h + 1], mx[:, h:h + 1], -SCALE, nsink[:, h:h + 1], ALU.mult, ALU.min).then_inc(s_nm.sem, 1)
                    if h == NH - 1:
                        dve.wait_ge(s_nm.sem, s_nm.at(l, i + 1))
                        V.tensor_tensor(esum[:, :], sinkb[:, :], nmx[:, t % 2, :], ALU.add).then_inc(s_esum.sem, 1)
                    copy_pt(i - 1)
                    if h == 2 and t >= 1:
                        normalise(t - 1)
                copy_pt(len(S) - 1)
                normalise(NT[l] - 1)
                dve.wait_ge(s_g1.sem, s_g1.at(l, 16 * (NT[l] // 2)))
                dve.wait_ge(s_a2.sem, s_a2.at(l, 16 * (NT[l] + 1)))
                for s in range(NT[l] // 2):
                    sc2 = work(l, 2048 * s, 1024)
                    link(V.scalar_tensor_tensor(out=sc2, in0=sc2, scalar=1.0, in1=vbuf[:, :], op0=ALU.add, op1=ALU.mult))

                def rows2(t):
                    s = t // NX
                    dve.wait_ge(s_r2.sem, s_r2.at(l, t + 1))
                    link(V.scalar_tensor_tensor(out=h2[:, t, :], in0=xres[:, t, :], scalar=st[:, 3, t:t + 1], in1=work(l, 2048 * s, 1024),
                                                op0=ALU.mult, op1=ALU.mult))
                    V.tensor_tensor(h2[:, t, :], h2[:, t, :], work(l, 2048 * s + 1024, 1024), ALU.add).then_inc(s_h2.sem, 1)

                def columns2(t):
                    dve.wait_ge(s_h2p.sem, s_h2p.at(l, 2 * t + 2))
                    if t >= 2:
                        dve.wait_ge(s_lq.sem, s_lq.at(l, t - 1))
                    V.tensor_copy(hr(l, t % 2)[:, 512:1024], pb[5 + 2 * (t % 2)][:, :]).then_inc(s_h2V.sem, 1)

                for t in range(NT[l]):
                    s = t // NX
                    g1 = cz(l).rearrange("p j t -> p (j t)") if s == 0 else ybuf[:, :]
                    for hf in range(2):
                        n = 2 * t + hf
                        half = slice(hf * 512, (hf + 1) * 512)
                        tmp = h2[:, t, half]
                        dve.wait_ge(s_op.sem, s_op.at(l, n + 1))
                        V.tensor_tensor(tmp, pb[2 + n % 2][:, :], g1[:, half], ALU.mult).then_inc(s_og.sem, 1)
                        dve.wait_ge(s_og.sem, s_og.at(l, n + 1))
                        V.tensor_tensor(xres[:, t, half], xres[:, t, half], tmp, ALU.add).then_inc(s_ox.sem, 1)
                        dve.wait_ge(s_ox.sem, s_ox.at(l, n + 1))
                        if t >= 1 and hf == 0:
                            columns2(t - 1)
                    rows2(t)
                columns2(NT[l] - 1)

                T_, B = NT[l], NT[l] * NE // 4
                W = NT[l] * NE
                ra = lambda i, m=64: work(l, rt0 + 64 * i, m)
                score_, sel, kept, gate, posm, himask = (ra(i) for i in range(6))
                chosen = chosen_experts(l)
                cmp_ = ra(8, 256)
                gsum, gone = ra(7)[:, 0:16], ra(7)[:, 16:32]
                nt_e, red = ra(12)[:, 16:32], ra(12)[:, 32:64]
                start_ = ra(13)[:, 0:NE + 1]
                pref = qkbuf[:, 0:(NE + 1) * NE]
                V.memset(cmp_, 0.0)
                link(V.memset(chosen[:, W:W + NE], 0.0))
                dve.wait_ge(s_sig.sem, s_sig.at(l, 1))
                t3 = lambda ap: ap[:, 0:W].rearrange("p (t e) -> p t e", e=NE)

                def rank(dst, src, nb):
                    c4 = cmp_[:, 0:nb * 16].rearrange("p (b i j) -> p b i j", i=4, j=4)
                    v = src[:, 0:nb * 4].rearrange("p (b j) -> p b j", j=4)
                    for i in range(4):
                        if i > 0:
                            ins = V.tensor_tensor(c4[:, :, i, 0:i], v[:, :, i:i + 1].broadcast_to([P, nb, i]), v[:, :, 0:i], ALU.is_gt)
                        if i < 3:
                            ins = V.tensor_tensor(c4[:, :, i, i + 1:4], v[:, :, i:i + 1].broadcast_to([P, nb, 3 - i]), v[:, :, i + 1:4], ALU.is_ge)
                    link(ins)
                    link(V.tensor_reduce(dst[:, 0:nb * 4].rearrange("p (b j) -> p b j", j=4), c4.rearrange("p b i j -> p b j i"),
                                         AX, ALU.add))

                link(V.tensor_tensor(t3(sel), t3(score_), rbb[:, :].unsqueeze(1).broadcast_to([P, T_, NE]), ALU.add))
                rank(kept, sel, B)
                link(V.scalar_tensor_tensor(out=posm[:, 0:W], in0=kept[:, 0:W], scalar=2.0, in1=sel[:, 0:W], op0=ALU.is_lt, op1=ALU.mult))
                link(V.tensor_reduce(gsum[:, 0:B], posm[:, 0:W].rearrange("p (b j) -> p b j", j=4), AX, ALU.add))
                rank(gone, gsum, T_)
                link(V.tensor_scalar(gone[:, 0:B], gone[:, 0:B], 1.0, None, ALU.is_lt))
                V.scalar_tensor_tensor(out=chosen[:, 0:W].rearrange("p (b j) -> p b j", j=4), in0=kept[:, 0:W].rearrange("p (b j) -> p b j", j=4),
                                       scalar=2.0, in1=gone[:, 0:B].unsqueeze(2).broadcast_to([P, B, 4]),
                                       op0=ALU.is_lt, op1=ALU.mult).then_inc(s_msk.sem, 1)
                dve.wait_ge(s_msk.sem, s_msk.at(l, 1))
                link(V.tensor_tensor(gate[:, 0:W], chosen[:, 0:W], score_[:, 0:W], ALU.mult))
                link(V.tensor_reduce(red[:, 0:T_], t3(gate), AX, ALU.add))
                link(V.reciprocal(red[:, 0:T_], red[:, 0:T_]))
                link(V.tensor_tensor(t3(gate), t3(gate), red[:, 0:T_].unsqueeze(2).broadcast_to([P, T_, NE]), ALU.mult))
                dve.wait_ge(s_pre.sem, s_pre.at(l, 1))
                k8 = cst[:, C_COUNT + 1:C_COUNT + NT[l] * P // SLOTS]
                nk = NT[l] * P // SLOTS - 1
                more = cmp_[:, 0:NE * nk].rearrange("p (e k) -> p e k", k=nk)
                link(V.scalar_tensor_tensor(out=more, in0=k8.unsqueeze(1).broadcast_to([P, NE, nk]), scalar=float(SLOTS),
                                            in1=pb[1][:, W:W + NE].unsqueeze(2).broadcast_to([P, NE, nk]), op0=ALU.mult, op1=ALU.is_lt))
                link(V.tensor_reduce(nt_e, more, AX, ALU.add))
                dve.wait_ge(s_rc.sem, s_rc.at(l, 16))
                pf3 = pref.rearrange("p (a b) -> p a b", b=NE)
                rc3 = work(l, 9216, 528)[:, R_PREFIX:R_PREFIX + (NE + 1) * NE].rearrange("p (a b) -> p a b", b=NE)
                link(V.scalar_tensor_tensor(out=pf3, in0=nt_e.unsqueeze(1).broadcast_to([P, NE + 1, NE]), scalar=1.0, in1=rc3,
                                            op0=ALU.add, op1=ALU.mult))
                link(V.tensor_reduce(start_, pf3, AX, ALU.add))
                V.tensor_copy(tab[l][0:1, 0:NE + 1], start_[0:1, :])
                V.tensor_scalar(tab[l][0:1, NE + 1:NE + 2], start_[0:1, NE:NE + 1], -1.0, float(NTILE), ALU.mult, ALU.add)
                link(V.scalar_tensor_tensor(out=t3(posm), in0=start_[:, 0:NE].unsqueeze(1).broadcast_to([P, T_, NE]), scalar=float(SLOTS),
                                            in1=t3(pb[1][:, :]), op0=ALU.mult, op1=ALU.add))
                link(V.scalar_tensor_tensor(out=posm[:, 0:W], in0=posm[:, 0:W], scalar=1.0, in1=chosen[:, 0:W], op0=ALU.add, op1=ALU.mult))
                link(V.tensor_reduce(posf[:, 1, 0:T_], t3(posm), AX, ALU.max))
                link(V.tensor_reduce(posf[:, 0, 0:T_], t3(posm), AX, ALU.add))
                link(V.tensor_tensor(t3(himask), t3(posm), posf[:, 1, 0:T_].unsqueeze(2).broadcast_to([P, T_, NE]), ALU.is_equal))
                link(V.tensor_tensor(posf[:, 0, 0:T_], posf[:, 0, 0:T_], posf[:, 1, 0:T_], ALU.subtract))
                V.tensor_scalar(posi[:, :, 0:T_], posf[:, :, 0:T_], -1.0, None, ALU.add).then_inc(s_slot.sem, 1)
                dve.wait_ge(s_slot.sem, s_slot.at(l, 1))
                link(V.tensor_tensor(posm[:, 0:W], himask[:, 0:W], gate[:, 0:W], ALU.mult))
                link(V.tensor_tensor(gate[:, 0:W], gate[:, 0:W], posm[:, 0:W], ALU.subtract))
                link(V.tensor_reduce(wtk[:, 1, 0:T_], t3(posm), AX, ALU.add))
                V.tensor_reduce(wtk[:, 0, 0:T_], t3(gate), AX, ALU.add).then_inc(s_pos.sem, 1)

                def copy_rows(count):
                    dve.wait_ge(s_hTp[l], count)
                    V.tensor_copy(hTe, pb[5][:, :].rearrange("p (k s) -> p k s", k=KD)).then_inc(s_hT[l], 1)

                dve.wait_ge(s_pos.sem, s_pos.at(l, 1))
                total = dve.value_load(tab[l][0:1, NE:NE + 1], min_val=NE, max_val=NTILE - 1)
                copy_rows(1)
                with dve.Fori(0, total) as T:
                    for hf in range(2):
                        dve.wait_ge(s_si[l], T * 2 + (hf + 1))
                        V.tensor_tensor(ae[:, hf * 256:(hf + 1) * 256], sg[:, hf * 256:(hf + 1) * 256], pb[hf][SLOTS:P, 0:256],
                                        ALU.mult).then_inc(s_a[l], 1)
                        dve.wait_ge(s_at[l], T * 2 + (hf + 1))
                        V.tensor_copy(aTe[:, 2 * hf:2 * hf + 2, :], pb[2 + hf][:, 0:2 * SLOTS].rearrange("p (k s) -> p k s", k=2)).then_inc(s_aT[l], 1)
                    copy_rows(T + 2)
                dve.wait_ge(s_g2.sem, s_g2.at(l, 16 * (NT[l] // 2)))
                for t in range(NT[l]):
                    dve.wait_ge(s_yg[t % 3].sem, s_yg[t % 3].at(l, 32 * (t // 3 + 1)))
                    dve.wait_ge(s_yl.sem, s_yl.at(l, t + 1))
                    lo, hi = ybuf2(t, 0), ybuf2(t, 1)
                    g2 = vbuf[:, :] if t < NX else ybuf[:, :]
                    link(V.scalar_tensor_tensor(out=lo, in0=hi, scalar=wtk[:, 1, t:t + 1], in1=lo, op0=ALU.mult, op1=ALU.add))
                    link(V.tensor_tensor(lo, lo, g2, ALU.mult))
                    V.tensor_tensor(xres[:, t, :], xres[:, t, :], lo, ALU.add).then_inc(s_comb.sem, 1)
                    if l + 1 < DEPTH and 1 <= t <= 2:
                        rows1(l + 1, t - 1)
                dve.wait_ge(s_comb.sem, s_comb.at(l, NT[l]))
            l = DEPTH - 1
            dve.wait_ge(s_fg, 16)
            for t in range(NX):
                dve.wait_ge(s_rf, t + 1)
                V.scalar_tensor_tensor(out=hr(l, t), in0=xres[:, t, :], scalar=st[:, 1, t:t + 1], in1=qtbuf[:, 0:D],
                                       op0=ALU.mult, op1=ALU.mult).then_inc(s_fin, 1)


def norm1_evac(nc, act, l, t, s_ta, s_tA, pb, ht, a1t, mt, mtc, nx):
    act.wait_ge(s_ta.sem, s_ta.at(l, 2 * t + 1))
    s = t // nx
    for k in range(4):
        b0 = mtc["sh1", s] + k
        ins = nc.scalar.activation(ht[:, k, t * P:(t + 1) * P], pb[4 + (2 * t) % 4][:, k * P:(k + 1) * P], ACT.Identity,
                                   scale=a1t[:, s, k:k + 1], bias=mt[:, b0:b0 + 1])
    ins.then_inc(s_tA.sem, 1)


_INS = ["x", "c", "ctx", "c_ctx", "w_mod", "b_mod", "norm1_g", "norm2_g", "w_in", "gmlp_g", "w_s", "b_s", "conv_w",
        "attn_sink", "w_out", "router_w", "router_b", "w_gate", "w_up", "w_down", "final_g"]
_OUTS = [((1, 256, 1024), "float32")]


def kernel(**inputs):
    import numpy as _np
    import concourse.bacc as _bacc
    from concourse import mybir as _mybir
    from concourse.bass_utils import run_bass_kernel_spmd as _run

    nc = _bacc.Bacc("TRN2", target_bir_lowering=False, num_devices=1)
    given = {name: _np.ascontiguousarray(inputs[name]) for name in _INS}
    given["consts"] = shape_constants(64)
    given["rconsts"] = router_constants(given["router_w"].shape[1])
    arrays, args = {}, []
    for name, a in given.items():
        arrays[f"in_{name}_dram"] = a
        args.append(nc.dram_tensor(f"in_{name}_dram", a.shape, _mybir.dt.from_np(a.dtype), kind="ExternalInput").ap())
    for i, (shape, dtype) in enumerate(_OUTS):
        dt = _mybir.dt.from_np(_np.dtype(dtype))
        args.append(nc.dram_tensor(f"out_{i}_dram", shape, dt, kind="ExternalOutput").ap())
    hybrid_trunk(nc, *args)
    r = _run(nc, [arrays], core_ids=[0])
    got = tuple(r.results[0][f"out_{i}_dram"] for i in range(len(_OUTS)))
    return got[0]
```

```python
from contextlib import ExitStack

import numpy as np

import concourse.bass as bass
from concourse import mybir

F32 = mybir.dt.float32
I32 = mybir.dt.int32
U32 = mybir.dt.uint32
ALU = mybir.AluOpType
ACT = mybir.ActivationFunctionType
AX = mybir.AxisListType.X

P = 128
MB = 1 << 20
EPS = 1e-6
GRID_W = 64
ROPE_BASE = 10000.0
SLOTS = 64
RING = 3
MASKED = -1e30

C_ID, C_COS, C_SIN, C_MASK, C_FOLD, C_COUNT = 0, 128, 256, 384, 640, 656
N_CONST = 724
R_BEFORE, R_ONES, R_PREFIX = 0, 128, 256


def shape_constants(head_dim):
    quarter = head_dim // 4
    tok = np.arange(2 * P, dtype=np.float32)
    inv = (ROPE_BASE ** (-np.arange(quarter, dtype=np.float32) / quarter)).astype(np.float32)
    ang = np.stack([np.floor(tok / GRID_W)[:, None] * inv, (tok % GRID_W)[:, None] * inv], axis=1)
    cos, sin = np.cos(ang), np.sin(ang)
    cos2 = np.stack([cos, cos], axis=2).reshape(2, P, head_dim)
    sin2 = np.stack([-sin, sin], axis=2).reshape(2, P, head_dim)
    i, j = np.arange(P)[:, None], np.arange(P)[None, :]
    consts = np.concatenate([
        np.eye(P), cos2[0], cos2[1], sin2[0], sin2[1],
        np.where(j > i, MASKED, 0.0), np.where(i > j, MASKED, 0.0),
        (i % 32 == np.arange(16)), np.tile(np.arange(SLOTS + 4), (P, 1)),
    ], axis=1).astype(np.float32)
    return consts


def router_constants(n_experts):
    i, j = np.arange(P)[:, None], np.arange(P)[None, :]
    before = (np.arange(n_experts)[None, :] < np.arange(n_experts + 1)[:, None]).reshape(1, -1)
    return np.concatenate([i < j, np.ones((P, P)), np.tile(before, (P, 1))], axis=1).astype(np.float32)


class Stage:

    def __init__(self, sem, total):
        self.sem, self.total = sem, total

    def at(self, layer, n):
        return layer * self.total + n


class Window:

    def __init__(self, eng, limit):
        self.eng, self.limit, self.flying = eng, limit, []

    def room(self, nbytes):
        while self.flying and sum(n for n, _, _ in self.flying) + nbytes > self.limit:
            _, sem, value = self.flying.pop(0)
            self.eng.wait_ge(sem, value)

    def started(self, nbytes, sem, value):
        self.flying.append((nbytes, sem, value))


class Tally:

    def __init__(self, eng, sem):
        self.eng, self.sem, self.n = eng, sem, 0

    def inc(self, ins):
        ins.then_inc(self.sem, 1)
        self.n += 1
        return self.n

    def link(self, ins):
        self.eng.wait_ge(self.sem, self.inc(ins))


def hybrid_trunk(nc, x, c, ctx, c_ctx, w_mod, b_mod, norm1_g, norm2_g, w_in, gmlp_g, w_s, b_s,
                 conv_w, attn_sink, w_out, router_w, router_b, w_gate, w_up, w_down, final_g,
                 consts, rconsts, out):
    DEPTH, D, _ = w_mod.shape
    KD = D // P
    W_A = gmlp_g.shape[1]
    A_GROUPS = w_s.shape[1]
    NH = attn_sink.shape[1]
    HD = 64
    NKV = 2
    W_C = NH * HD
    W_B = conv_w.shape[2]
    COL_U, COL_V, COL_B, COL_C, COL_Z = 0, W_A, 2 * W_A, 2 * W_A + W_B, 2 * W_A + 2 * W_B
    COL_Q = 2 * W_A + 3 * W_B
    COL_K = COL_Q + W_C
    IN_COLS = w_in.shape[2]
    KV2 = IN_COLS - COL_K
    SCALE = HD ** -0.5
    NE = w_gate.shape[1]
    FE = w_gate.shape[3]
    KF = FE // P
    NX, NALL = 2, 4
    MODW = 6 * D
    NTILE = 2 * NALL * P // SLOTS + NE
    NP = 6 * DEPTH
    HK = KD // 2
    MH = D // 2
    FIRST = 4
    NT = [NALL if l < DEPTH - 1 else NX for l in range(DEPTH)]

    es = ExitStack()
    with es:
        def sb(name, shape, dt=F32):
            return es.enter_context(nc.sbuf_tensor(name, shape, dt))

        def sem(name):
            return es.enter_context(nc.semaphore(name))

        def lsem(name):
            return [sem(f"{name}_{l}") for l in range(DEPTH)]

        mod_d = nc.dram_tensor("mod_rows", [DEPTH, 2, MODW], F32).ap()
        hsort = nc.dram_tensor("h_by_expert", [NTILE * SLOTS, D], F32).ap()
        ysort = nc.dram_tensor("y_by_expert", [NTILE * SLOTS, D], F32).ap()

        SLOT = 2 * KD * FE + KF * D
        big = sb("weight_ring", [P, RING * SLOT])
        xres = sb("residual", [P, NALL, D])
        ybuf = sb("conv_y", [P, D])
        vbuf = sb("gmlp_v", [P, D])
        qkbuf = sb("qk_tokens", [P, NALL * (W_C + 256) + NALL * P])
        qtbuf = sb("q_k_transposed", [P, 4096])
        cst = sb("consts_sb", [P, N_CONST])
        mrow = sb("modulation_sums", [P, MH])
        esum = sb("sink_minus_max", [P, NH])
        wst = sb("w_s_transposed", [P, A_GROUPS, P])
        bsb = sb("b_s_rows", [P, 2, P])
        rwb = sb("router_w_sb", [P, KD, NE])
        mt = sb("layer_columns", [P, 32])
        modt = sb("shift_scale_columns", [P, DEPTH, 2, 2, KD])
        sht = sb("norm1_shift", [P, 2, KD])
        a1t = sb("norm1_scale", [P, 2, KD])
        a1s = sb("scale_with_bias", [P, 2, KD])
        sinkb = sb("sink_rows", [P, NH])
        nsink = sb("minus_sink", [P, NH])
        rbb = sb("router_b_rows", [P, NE])
        st = sb("row_stats", [P, 6, NALL + 1])
        mx = sb("score_max", [P, NH])
        nmx = sb("minus_max", [P, 2, NH])
        rsum = sb("prob_sum", [P, 2, NH])
        esink = sb("sink_prob", [P, NH])
        rden = sb("inverse_sum", [P, NH])
        posf = sb("slot_numbers_f", [P, 2, NALL])
        posi = sb("slot_numbers", [P, 2, NALL], I32)
        wtk = sb("gate_weights", [P, 2, NALL])
        tab = [sb(f"first_tile_{l}", [1, 32], I32) for l in range(DEPTH)]

        def slot(n, a=0, m=SLOT):
            return big[:, (n % RING) * SLOT + a:(n % RING) * SLOT + a + m]

        def wgate(n):
            return slot(n, 0, KD * FE).rearrange("p (k f) -> p k f", k=KD)

        def wup(n):
            return slot(n, KD * FE, KD * FE).rearrange("p (k f) -> p k f", k=KD)

        def wdown(n):
            return slot(n, 2 * KD * FE, KF * D).rearrange("p (k f) -> p k f", k=KF)

        def win(l, kind):
            off, n = KD * win_at[kind], cols_of[kind][1]
            return big[:, l * SLOT + off:l * SLOT + off + KD * n].rearrange("p (k f) -> p k f", k=KD)

        def wout(l):
            a = l * SLOT + KD * IN_COLS
            return big[:, a:a + KD * D].rearrange("p (h k f) -> p h k f", h=2, k=KD)

        def work(l, a, m):
            return slot(l + 2, a, m)

        def ht(l):
            return work(l, 0, 4096).rearrange("p (k t) -> p k t", k=KD)

        def mixt(l):
            return work(l, 4096, KD * NT[l] * P).rearrange("p (k t) -> p k t", k=KD)

        def scale2(l, s):
            return work(l, 2048 * s if NT[l] == NALL else 6144, 1024)

        def shift2(l, s):
            return work(l, (2048 * s if NT[l] == NALL else 6144) + 1024, 1024)

        def cz(l):
            return work(l, 8192, 1024).rearrange("p (j t) -> p j t", j=2)

        def ropet(l):
            return work(l, 9216, 768)

        sct = work(0, 9984, 256).rearrange("p (k m) -> p k m", k=KD)

        def hr(l, i):
            return work(l, 10240 + 1024 * i, 1024)

        def prob(l, i):
            return work(l, 10240 + 512 * i, 512)

        def probt(l, i):
            return work(l, 11264 + 512 * i, 512).rearrange("p (k q) -> p k q", k=4)

        def wmodbuf(m):
            a = {2: 2 * SLOT + 4096, 3: KD * win_at["b"]}.get(m, KD * IN_COLS + (m % 2) * HK * D)
            return big[:, a:a + HK * D].rearrange("p (k n) -> p k n", k=HK)

        def ybuf2(t, k):
            if t == NALL - 1:
                return qkbuf[:, 1536 + 1024 * k:2560 + 1024 * k]
            a = 4096 + 1024 * (2 * t + k)
            return big[:, a:a + 1024]

        rt0 = 8192

        def chosen_experts(l):
            return work(l, rt0 + 896, (NALL + 1) * NE)

        def logit_quarters(l):
            return work(l, 9744, P)

        QW = W_C + 256
        qk = qkbuf[:, 0:NALL * QW].rearrange("p (t n) -> p t n", t=NALL)
        vv = qkbuf[:, NALL * QW:NALL * QW + NALL * P].rearrange("p (t n) -> p t n", t=NALL)
        vt = vbuf[:, :].rearrange("p (t n) -> p t n", t=NALL)
        yc = ybuf[:, :].rearrange("p (j t) -> p j t", j=2)
        rows = qtbuf[:, 0:P]
        ws_raw = qtbuf[:, P:P + 512].rearrange("p (h q) -> p h q", h=A_GROUPS)
        qT = qtbuf[:, 0:2048].rearrange("p (b t) -> p b t", b=4)
        kz = qtbuf[:, 2048:4096].rearrange("p (z v t) -> p z v t", z=2, v=NKV)
        h2 = qtbuf[:, :].rearrange("p (t n) -> p t n", t=NALL)
        hrow = qkbuf[0:SLOTS, 0:1024]
        hTe = qkbuf[:, 1024:1536].rearrange("p (k s) -> p k s", k=KD)
        sg = qkbuf[SLOTS:P, 1536:2048]
        ae = qkbuf[0:SLOTS, 2048:2560]
        aTe = qkbuf[:, 2560:2816].rearrange("p (k s) -> p k s", k=KF)
        ysb = qkbuf[:, 2816:3328]
        picked = qkbuf[:, 2560:2816].rearrange("p (t s) -> p t s", t=NALL)
        same = qkbuf[:, 2816:3328].rearrange("p (k t s) -> p k t s", k=2, t=NALL)
        ident = cst[:, C_ID:C_ID + P]

        pb = [es.enter_context(nc.psum_tensor(f"bank{i}", [P, 512], F32)) for i in range(8)]

        s_const = sem('s_const')
        s_rw = sem('s_router_weights')
        s_cvec = sem('s_cvec')
        s_x = [sem('s_x'), sem('s_ctx')]
        s_sctz = sem('s_sct_zeroed')
        s_ctp = sem('s_c_transposed')
        s_sct = sem('s_sct')
        s_wm = [sem(f"s_wmod_{i}") for i in range(4)]
        s_binit, s_modpe = sem("s_bmod_rows"), sem("s_modpe")
        s_modw = [sem("s_modstored_even"), sem("s_modstored_odd")]
        s_mh, s_mr = sem("s_mod_half_copied"), sem("s_mod_summed")
        s_modt, s_modtc = sem("s_modturned"), sem("s_modturned_copied")
        s_esum = Stage(sem("s_sink_minus_max"), 4)
        s_row = Stage(sem("s_rows"), 64)
        s_small = Stage(sem("s_small"), 96)
        s_mtp = Stage(sem("s_mtp"), 1)
        s_mt = Stage(sem("s_mt"), 1)
        s_wsp = Stage(sem("s_wsp"), 1)
        s_wst = Stage(sem("s_wst"), 1)
        s_ss = Stage(sem("s_ss"), 4)
        s_hr = Stage(sem("s_hr"), 4)
        s_ta = Stage(sem("s_ta"), 8)
        s_tA = Stage(sem("s_tA"), 4)
        s_tV = Stage(sem("s_tV"), 4)
        s_hmA, s_hmV = sem("s_modulatedA"), sem("s_modulatedV")
        GROUPS = ['q', 'kv', 'v', 'c', 'z', 'b', 'u']
        s_win = {g: Stage(sem(f's_win_{g}'), 16) for g in GROUPS}
        s_wout = [Stage(sem(f"s_wout_{hf}"), 16) for hf in range(2)]
        s_pj = Stage(sem("s_proj"), 20)
        s_pA = Stage(sem("s_projA"), 14)
        s_pV = Stage(sem("s_projV"), 6)
        s_kz = Stage(sem("s_kz"), 1)
        s_rope = Stage(sem("s_rope"), 2)
        s_qtp = Stage(sem("s_qtp"), 4)
        s_qtA = Stage(sem("s_qtA"), 4)
        s_qtV = Stage(sem("s_qtV"), 4)
        s_vn = Stage(sem("s_vn"), 4)
        s_gp = Stage(sem("s_gatep"), 2)
        s_gm = Stage(sem("s_gmlp"), 4)
        s_conv = Stage(sem("s_conv"), 2)
        s_nsink = Stage(sem("s_nsink"), 1)
        s_sc = Stage(sem("s_scores"), 32)
        s_nm = Stage(sem("s_max"), 32)
        s_ex = Stage(sem("s_exp"), 32)
        s_es = Stage(sem("s_expsink"), 4)
        s_pt = Stage(sem("s_probT"), 32)
        s_ptA = Stage(sem("s_probTA"), 16)
        s_ptV = Stage(sem("s_probTV"), 16)
        s_pv = Stage(sem("s_pv"), 32)
        s_on = Stage(sem("s_attn"), 4)
        s_ot = Stage(sem("s_attnT"), 4)
        s_om = Stage(sem("s_attn_mix"), 4)
        s_g1 = Stage(sem("s_g1"), 32)
        s_op = Stage(sem("s_outp"), 8)
        s_og = Stage(sem("s_outg"), 8)
        s_ox = Stage(sem("s_outx"), 8)
        s_a2 = Stage(sem("s_a2"), 80)
        s_ss2 = Stage(sem("s_ss2"), 4)
        s_h2 = Stage(sem("s_h2"), 4)
        s_h2p = Stage(sem("s_h2T"), 8)
        s_h2A = Stage(sem("s_h2TA"), 4)
        s_h2V = Stage(sem("s_h2TV"), 4)
        s_rc = Stage(sem("s_rconst"), 16)
        s_lq = Stage(sem("s_logit_quarters"), 4)
        s_lqc = Stage(sem("s_logit_quarters_copied"), 4)
        s_lg = Stage(sem("s_logits"), 4)
        s_sig = Stage(sem("s_sigmoid"), 1)
        s_msk = Stage(sem("s_mask"), 1)
        s_pre = Stage(sem("s_prefix"), 1)
        s_slot = Stage(sem("s_slot_numbers"), 1)
        s_pos = Stage(sem("s_pos"), 1)
        s_zeros = sem('s_zeros')
        s_hz = sem('s_hsort_zero')
        s_scat = Stage(sem("s_scatter"), 128)
        GATE, UP, DOWN = (0, 2), (1, 3), (4, 5)
        s_we = [[sem(f"s_expert_{r}_{i}") for i in range(6)] for r in range(RING)]

        def weights_at(l, r, use):
            return (l * len(range(r, NE, RING)) + use) * 16

        s_pick = Stage(sem('s_first_rows_picked'), 1)
        s_hrow = lsem('s_hrow')
        s_hTp = lsem('s_hTp')
        s_hT = lsem('s_hT')
        s_gu = lsem('s_gateup')
        s_si = lsem('s_silu')
        s_a = lsem('s_a')
        s_at = lsem('s_aTp')
        s_aT = lsem('s_aT')
        s_d = lsem('s_down')
        s_y = lsem('s_y')
        s_yd = lsem('s_ystored')
        s_g2 = Stage(sem("s_g2"), 32)
        s_yg = [Stage(sem(f"s_ygather_{t}"), 32) for t in range(NALL)]
        s_yl = Stage(sem("s_ylow_scaled"), 4)
        s_comb = Stage(sem("s_combined"), 4)
        s_fg = sem('s_final_g')
        s_ssf = sem('s_ss_final')
        s_fin = sem('s_final')
        s_out = sem('s_out')
        s_r1, s_r2, s_vs, s_rv = (Stage(sem(n), 4) for n in ("s_root1", "s_root2", "s_vsum", "s_rootv"))
        s_rf = sem("s_root_final")
        s_yz = sem("s_ysort_rest")
        s_pl = sem("s_pool_chain")
        s_passed, s_pool_passed = sem("s_passed"), sem("s_pool_passed")
        s_dv = sem("s_dve_chain")

        def proj_jobs(l):
            if l == 0:
                jobs = [("q", t, "A") for t in range(NT[l])] + [("kv", t, "V") for t in range(NALL)]
            else:
                jobs = [job for t in range(NALL) for job in ([("q", t, "A")] if t < NT[l] else []) + [("kv", t, "V")]]
            jobs += [("v", t, "A") for t in range(NT[l])]
            jobs += [("c", j, "A") for j in range(2)] + [("z", j, "V") for j in range(2)]
            jobs += [("b", j, "A") for j in range(2)] + [("u", j, "A") for j in range(2)]
            return jobs

        win_at = {"q": 0, "kv": W_C, "v": W_C + KV2, "c": W_C + KV2 + W_A, "z": W_C + KV2 + W_A + W_B,
                  "b": W_C + KV2 + W_A + 2 * W_B, "u": W_C + KV2 + W_A + 3 * W_B}

        MOD_JOBS = {0: 4, 1: 5, 2: 6, 3: 7, 5: 8, 7: 9, 9: 10, 11: 11, 12: 12, 13: 13, 14: 14, 15: 15,
                    16: 16, 17: 17, 18: 18, 19: 19}
        MOD_STEPS = {3: 20, 7: 21, 11: 22, 15: 23}

        def mod_bank(piece):
            return pb[piece if piece < 2 else 4 + piece % 2 if piece < 10 else 3]

        def turned(piece):
            return piece % 6 < 2

        def n_turned(upto):
            return sum(turned(n) for n in range(upto))

        def n_stored(upto, parity):
            return sum(not turned(n) for n in range(parity, upto, 2))

        def evacuated(jobs, upto, eng):
            return sum(1 for j in jobs[:upto] if j[2] == eng)

        cols_of = {"q": (COL_Q, W_C), "kv": (COL_K, KV2), "v": (COL_V, W_A), "c": (COL_C, W_B),
                   "z": (COL_Z, W_B), "b": (COL_B, W_B), "u": (COL_U, W_A)}

        def steps(l):
            return [(t, h) for t in range(NT[l]) for h in range(NH)]

        def score_bank(i):
            return pb[(4, 5, 2)[i % 3]]

        def keys(t):
            return (0, 512) if t < NX else (256, 256)

        def pt_engine(i):
            return "A" if i % 2 == 0 else "V"

        def pt_count(i, eng):
            return i // 2 + 1 if eng == "A" else (i + 1) // 2

        MT_BIAS, MT_N1, MT_CONV, MT_GMLP = 0, 2 * KD, 3 * KD, 3 * KD + 6
        N_ROWS = MT_GMLP + 2

        def mod_part(l, s, n):
            return mod_d[l, s, n * D:(n + 1) * D].partition_broadcast(P)

        block = es.enter_context(nc.Block())

        @block.sync
        def _(sp):
            def load_mod(m):
                l, n, kh = m // 12, m // 2 % 6, m % 2
                if m >= FIRST:
                    sp.wait_ge(s_modpe, m - 1 if m > FIRST + 1 else FIRST)
                window.room(2 * MB)
                window.started(2 * MB, s_wm[m % 4], 16 * (m // 4 + 1))
                sp.dma_start(wmodbuf(m), w_mod[l, kh * HK * P:(kh + 1) * HK * P, n * D:(n + 1) * D]
                             .rearrange("(k p) n -> p k n", p=P)).then_inc(s_wm[m % 4], 16)

            def load_win(l, g):
                c0, n = cols_of[g]
                window.room(n * 4 * D)
                window.started(n * 4 * D, s_win[g].sem, s_win[g].at(l, 16))
                sp.dma_start(win(l, g), w_in[l, :, c0:c0 + n].rearrange("(k p) n -> p k n", p=P)).then_inc(s_win[g].sem, 16)

            def load_wout(l):
                for hf in range(2):
                    window.room(2 * MB)
                    window.started(2 * MB, s_wout[hf].sem, s_wout[hf].at(l, 16))
                    sp.dma_start(wout(l)[:, hf], w_out[l, :, hf * 512:(hf + 1) * 512].rearrange("(k p) n -> p k n", p=P)
                                 ).then_inc(s_wout[hf].sem, 16)

            def load_small(l):
                sp.dma_start(ws_raw, w_s[l].rearrange("h p q -> p h q")).then_inc(s_small.sem, 16)
                for h in range(A_GROUPS):
                    r = 64 * (h % 2)
                    sp.dma_start(bsb[r:r + 64, h // 2, :], b_s[l, h].partition_broadcast(64)).then_inc(s_small.sem, 16)
                sp.dma_start(sinkb[:, :], attn_sink[l].partition_broadcast(P)).then_inc(s_small.sem, 16)
                sp.dma_start(rows[0:MT_N1, :], b_mod[l, 0:2 * D].rearrange("(r p) -> r p", p=P)).then_inc(s_row.sem, 16)
                sp.dma_start(rows[MT_N1:MT_CONV, :], norm1_g[l].rearrange("(k p) -> k p", p=P)).then_inc(s_row.sem, 16)
                sp.dma_start(rows[MT_GMLP:N_ROWS, :], gmlp_g[l].rearrange("(j p) -> j p", p=P)).then_inc(s_row.sem, 16)
                sp.dma_start(rows[MT_CONV:MT_GMLP, :], conv_w[l].rearrange("w (j p) -> (w j) p", p=P)).then_inc(s_row.sem, 16)

            window = Window(sp, 4 * MB)

            def expert_parts(l, e, n):
                gate, up, down = (w_gate, wgate(n), KD), (w_up, wup(n), KD), (w_down, wdown(n), KF)
                for (w, d, k), hf in ((gate, 0), (up, 0), (gate, 1), (up, 1), (down, 0), (down, 1)):
                    rows_ = slice(hf * k // 2 * P, (hf + 1) * k // 2 * P)
                    src = (w[l, e, rows_, :].rearrange("(k p) n -> p k n", p=P) if isinstance(e, int)
                           else w[l, bass.ds(e, 1), rows_, :].rearrange("a (k p) n -> p (a k) n", p=P))
                    yield d[:, hf * k // 2:(hf + 1) * k // 2, :], src

            def load_expert(l, e, n, parts=range(6)):
                r = n % RING
                for i, (dst, src) in enumerate(expert_parts(l, e, n)):
                    if i not in parts:
                        continue
                    window.room(MB)
                    sp.dma_start(dst, src).then_inc(s_we[r][i], 16)
                    window.started(MB, s_we[r][i], weights_at(l, r, e // RING + 1))

            def load_expert_looped(l, e, n, use, first):
                r, q = n % RING, (n - 1) % RING
                before = use if n > l else use - 1
                for i, (dst, src) in enumerate(expert_parts(l, e, n)):
                    if i == 0:
                        sp.wait_ge(s_gu[l], first * 2)
                    elif i == 4:
                        sp.wait_ge(s_d[l], first)
                    if i < 3:
                        sp.wait_ge(s_we[q][i + 3], before * 16 + weights_at(l, q, 0))
                    else:
                        sp.wait_ge(s_we[r][i - 3], use * 16 + weights_at(l, r, 0))
                    sp.dma_start(dst, src).then_inc(s_we[r][i], 16)

            crow = work(0, 9216, 128)
            sp.dma_start(crow[0:KD, :], c.rearrange("a (k p) -> (a k) p", p=P)).then_inc(s_cvec, 16)
            sp.dma_start(crow[KD:2 * KD, :], c_ctx.rearrange("(k p) -> k p", p=P)).then_inc(s_cvec, 16)
            sp.dma_start(cst[:, :], consts).then_inc(s_const, 16)
            sp.dma_start(xres[:, 0:NX, :], x.rearrange("a (t p) d -> p (a t) d", p=P)).then_inc(s_x[0], 16)
            sp.dma_start(xres[:, NX:NALL, :], ctx.rearrange("a (t p) d -> p (a t) d", p=P)).then_inc(s_x[1], 16)
            load_mod(0)
            load_mod(1)
            load_small(0)
            load_mod(2)
            load_mod(3)
            load_win(0, "q")
            for l in range(DEPTH):
                for s in range(2):
                    sp.dma_start(mod_d[l, s, :], b_mod[l, :]).then_inc(s_binit, 16)
            load_win(0, "kv")
            sp.dma_start(rwb[:, :, :], router_w.rearrange("(k p) n -> p k n", p=P)).then_inc(s_rw, 16)
            sp.dma_start(rbb[:, :], router_b.partition_broadcast(P)).then_inc(s_rw, 16)
            m = FIRST
            for g in GROUPS[2:]:
                load_win(0, g)
                for _ in range(3):
                    load_mod(m)
                    m += 1
            load_mod(m)
            for l in range(DEPTH):
                sp.wait_ge(s_pj.sem, s_pj.at(l, 2 * NT[l] + NALL + 4))
                load_expert(l, 0, l)
                if l == 0:
                    for m in range(20, 24):
                        load_mod(m)
                    sp.wait_ge(s_modpe, 24)
                    load_wout(0)
                sp.wait_ge(s_pj.sem, s_pj.at(l, len(proj_jobs(l))))
                sp.wait_ge(s_conv.sem, s_conv.at(l, 2))
                for q in range(2):
                    sp.wait_ge(s_modw[q], 32 * n_stored(6 * l + 5, q))
                for s in range(NT[l] // 2):
                    dst = cz(l).rearrange("p j t -> p (j t)") if s == 0 else ybuf[:, :]
                    sp.dma_start(dst, mod_part(l, s, 2)).then_inc(s_g1.sem, 16)
                for s in range(NT[l] // 2):
                    sp.dma_start(scale2(l, s), mod_part(l, s, 4)).then_inc(s_a2.sem, 16)
                    sp.dma_start(shift2(l, s), mod_part(l, s, 3)).then_inc(s_a2.sem, 16)
                sp.wait_ge(s_gp.sem, s_gp.at(l, 2))
                sp.dma_start(vbuf[:, :], norm2_g[l].partition_broadcast(P)).then_inc(s_a2.sem, 16)
                sp.wait_ge(s_qtp.sem, s_qtp.at(l, NALL))
                sp.dma_start(work(l, 9216, 528), rconsts).then_inc(s_rc.sem, 16)
                load_expert(l, 1, l + 1, GATE)
                early = GATE if NT[l] < NALL else ()
                if early:
                    sp.wait_ge(s_gm.sem, s_gm.at(l, 4))
                    load_expert(l, 2, l + 2, early)
                sp.wait_ge(s_op.sem, s_op.at(l, NT[l]))
                load_expert(l, 1, l + 1, UP)
                sp.wait_ge(s_op.sem, s_op.at(l, 2 * NT[l]))
                load_expert(l, 1, l + 1, DOWN)
                sp.wait_ge(s_h2.sem, s_h2.at(l, NT[l]))
                sp.wait_ge(s_modw[1], 32 * n_stored(6 * l + 6, 1))
                for s in range(NT[l] // 2):
                    sp.dma_start(vbuf[:, :] if s == 0 else ybuf[:, :], mod_part(l, s, 5)).then_inc(s_g2.sem, 16)
                window.limit = 2 * MB
                load_expert(l, 2, l + 2, [i for i in range(4) if i not in early])
                sp.wait_ge(s_pos.sem, s_pos.at(l, 1))
                load_expert(l, 2, l + 2, DOWN)
                if l + 1 < DEPTH:
                    sp.wait_ge(s_hTp[l], 1)
                    sp.wait_ge(s_hrow[l], 16)
                    load_small(l + 1)
                window.limit = 4 * MB
                with sp.Fori(0, (NE - 1) // RING - 1) as i:
                    for j in range(RING):
                        first = sp.value_load(tab[l][0:1, bass.ds(i * RING + (j + 1), 1)], min_val=0, max_val=NTILE)
                        load_expert_looped(l, i * RING + (RING + j), l + j, i + 2, first)
                first = sp.value_load(tab[l][0:1, NE - 3:NE - 2], min_val=0, max_val=NTILE)
                load_expert_looped(l, NE - 1, l + (NE - 1) % RING, (NE - 1) // RING + 1, first)
                if l + 1 < DEPTH:
                    window.flying = [(MB, s_we[(NE - 1 + l) % RING][i], weights_at(l, (NE - 1 + l) % RING, (NE - 1) // RING + 1))
                                     for i in range(3, 6)]
                    first = sp.value_load(tab[l][0:1, NE - 2:NE - 1], min_val=0, max_val=NTILE)
                    sp.wait_ge(s_d[l], first)
                    for g in GROUPS[:2]:
                        load_win(l + 1, g)
                    sp.wait_ge(s_comb.sem, s_comb.at(l, NT[l]))
                    for g in GROUPS[2:]:
                        load_win(l + 1, g)
                    load_wout(l + 1)
                else:
                    sp.wait_ge(s_scat.sem, s_scat.at(l, 32 * NT[l]))
                    sp.dma_start(qtbuf[:, 0:D], final_g.partition_broadcast(P)).then_inc(s_fg, 16)
            for t in range(NX):
                sp.wait_ge(s_fin, t + 1)
                sp.dma_start(out[0, t * P:(t + 1) * P, :], hr(DEPTH - 1, t)).then_inc(s_out, 16)
            sp.wait_ge(s_out, 16 * NX)

        @block.gpsimd
        def _(pool):
            nc.gpsimd.memset(work(0, 9984, 256), 0.0).then_inc(s_sctz, 1)

            def store_mod(pieces):
                for n in pieces:
                    if turned(n):
                        continue
                    pool.wait_ge(s_mr, n + 1)
                    for s in range(2):
                        a = 64 * (n % 2) + s
                        pool.dma_start(mod_d[n // 6, s, (n % 6) * D:(n % 6 + 1) * D].rearrange("(h n) -> h n", h=2),
                                       mrow[a:a + 64 - s:32, :], accum_op=ALU.add).then_inc(s_modw[n % 2], 16)

            pl = Tally(pool, s_pl)

            def inv_root(dst, src, n):
                pl.link(nc.gpsimd.tensor_scalar(dst, src, 1.0 / n, EPS, ALU.mult, ALU.add))
                return nc.gpsimd.tensor_tensor(dst, dst, half, ALU.pow)

            half = st[:, 5, NALL:NALL + 1]
            pl.link(nc.gpsimd.memset(half, -0.5))

            for l in range(DEPTH):
                if l == 0:
                    nc.gpsimd.memset(qtbuf[:, 2048:4096], 0.0).then_inc(s_kz.sem, 1)
                for t in range(NALL):
                    pool.wait_ge(s_ss.sem, s_ss.at(l, t + 1))
                    inv_root(st[:, 1, t:t + 1], st[:, 0, t:t + 1], D).then_inc(s_r1.sem, 1)
                if l == 0:
                    pool.wait_ge(s_binit, 64)
                    store_mod(range(2, 4))
                for t in range(NT[l]):
                    pool.wait_ge(s_vs.sem, s_vs.at(l, t + 1))
                    inv_root(st[:, 5, t:t + 1], st[:, 4, t:t + 1], W_A).then_inc(s_rv.sem, 1)
                if l == 0:
                    store_mod(range(4, 10))
                    store_mod(range(10, 12))
                    zeros = qkbuf[SLOTS:P, 1024:2048]
                    pool.wait_ge(s_ot.sem, s_ot.at(0, NALL))
                    nc.gpsimd.memset(zeros, 0.0).then_inc(s_zeros, 1)
                    pool.wait_ge(s_zeros, 1)
                    for n in range(NTILE):
                        pool.dma_start(hsort[n * SLOTS:(n + 1) * SLOTS, :], zeros).then_inc(s_hz, 16)
                for t in range(NT[l]):
                    pool.wait_ge(s_ss2.sem, s_ss2.at(l, t + 1))
                    inv_root(st[:, 3, t:t + 1], st[:, 2, t:t + 1], D).then_inc(s_r2.sem, 1)
                if l == 0:
                    pool.wait_ge(s_hz, 16 * NTILE)
                pool.wait_ge(s_slot.sem, s_slot.at(l, 1))
                pool.sem_inc(s_pool_passed, 1)
                for t in range(NT[l]):
                    for k in range(2):
                        pool.indirect_dma_start(
                            out=hsort, out_offset=bass.IndirectOffsetOnAxis(ap=posi[:, k, t:t + 1].bitcast(U32), axis=0),
                            in_=h2[:, t, :], in_offset=None).then_inc(s_scat.sem, 16)
                pool.wait_ge(s_scat.sem, s_scat.at(l, 32 * NT[l]))
                pool.wait_ge(s_pos.sem, s_pos.at(l, 1))
                total = pool.value_load(tab[l][0:1, NE:NE + 1], min_val=NE, max_val=NTILE - 1)
                pool.dma_start(hrow, hsort[SLOTS:2 * SLOTS, :]).then_inc(s_hrow[l], 16)
                if l == 0:
                    lacking = pool.value_load(tab[l][0:1, NE + 1:NE + 2], min_val=1, max_val=NTILE - NE)
                    with pool.Fori(0, lacking) as i:
                        pool.dma_start(ysort[bass.ds((i * -1 + (NTILE - 1)) * SLOTS, SLOTS), :],
                                       hsort[bass.ds((i * -1 + (NTILE - 1)) * SLOTS, SLOTS), :]).then_inc(s_yz, 16)
                with pool.Fori(1, total) as T:
                    pool.wait_ge(s_hTp[l], T + 1)
                    pool.dma_start(hrow, hsort[bass.ds((T + 1) * SLOTS, SLOTS), :]).then_inc(s_hrow[l], 16)
                if l + 1 < DEPTH:
                    nc.gpsimd.memset(qtbuf[:, 2048:4096], 0.0).then_inc(s_kz.sem, 1)
                if l == 0:
                    pool.wait_ge(s_yz, lacking * 16)
                pool.wait_ge(s_hrow[l], total * 16)
                pool.wait_ge(s_yd[l], total * 32 + 32)
                pool.sem_inc(s_pool_passed, 1)
                for t in range(NT[l]):
                    for k in range(2):
                        pool.indirect_dma_start(
                            out=ybuf2(t, k), out_offset=None, in_=ysort,
                            in_offset=bass.IndirectOffsetOnAxis(ap=posi[:, k, t:t + 1].bitcast(U32), axis=0)).then_inc(s_yg[t].sem, 16)
            for t in range(NX):
                pool.wait_ge(s_ssf, t + 1)
                inv_root(st[:, 1, t:t + 1], st[:, 0, t:t + 1], D).then_inc(s_rf, 1)

        @block.scalar
        def _(act):
            def copy_mod(piece):
                act.wait_ge(s_modpe, 2 * piece + 2)
                if piece >= 2:
                    act.wait_ge(s_modt, n_turned(piece - 1))
                if n_stored(piece, piece % 2) > 0:
                    act.wait_ge(s_modw[piece % 2], 32 * n_stored(piece, piece % 2))
                a = 64 * (piece % 2)
                nc.scalar.copy(mrow[a:a + 64, :], mod_bank(piece)[64 - a:128 - a, :]).then_inc(s_mh, 1)

            def columns1(l, t):
                act.wait_ge(s_ta.sem, s_ta.at(l, 2 * t + 1))
                bank, s = pb[4 + (2 * t) % 4], t // NX
                if l == 0:
                    ins = nc.scalar.copy(ht(l)[:, 0:HK, t * P:(t + 1) * P], bank[:, :].rearrange("p (k t) -> p k t", k=HK))
                else:
                    for k in range(HK):
                        ins = nc.scalar.activation(ht(l)[:, k, t * P:(t + 1) * P], bank[:, k * P:(k + 1) * P], ACT.Identity,
                                                   scale=a1t[:, s, k:k + 1], bias=sht[:, s, k:k + 1])
                ins.then_inc(s_tA.sem, 1)

            def copy_turned(piece):
                act.wait_ge(s_modt, n_turned(piece + 1))
                for s in range(2):
                    ins = nc.scalar.copy(modt[:, piece // 6, piece % 6, s, :].rearrange("p (h b) -> p h b", h=2),
                                         mod_bank(piece)[:, :].rearrange("p (b q h r) -> p q h b r", b=4, q=2, h=2)[:, piece % 2, :, :, s])
                ins.then_inc(s_modtc, 1)

            def scale_low(l, t):
                act.wait_ge(s_yg[t].sem, s_yg[t].at(l, 32))
                nc.scalar.activation(ybuf2(t, 0), ybuf2(t, 0), ACT.Copy, scale=wtk[:, 0, t:t + 1]).then_inc(s_yl.sem, 1)

            act.wait_ge(s_sctz, 1)
            act.wait_ge(s_ctp, 1)
            nc.scalar.activation(sct[:, :, 0:2], pb[0][:, 0:16].rearrange("p (s k) -> p k s", s=2), ACT.Silu).then_inc(s_sct, 1)
            for l in range(DEPTH):
                for t in range(NALL):
                    if l > 0:
                        act.wait_ge(s_comb.sem, s_comb.at(l - 1, t + 1))
                    elif t in (0, NX):
                        act.wait_ge(s_x[t // NX], 16)
                    if t >= 2:
                        act.wait_ge(s_ta.sem, s_ta.at(l, 2 * (t - 1)))
                    nc.scalar.activation(hr(l, t % 2), xres[:, t, :], ACT.Square, accum_out=st[:, 0, t:t + 1]).then_inc(s_ss.sem, 1)
                    if l > 0 and t == 0:
                        scale_low(l - 1, 2)
                        act.wait_ge(s_mt.sem, s_mt.at(l, 1))
                        columns1(l, 0)
                    elif l > 0 and t == 1:
                        scale_low(l - 1, 3)
                    elif t >= 1:
                        columns1(l, t - 1)
                columns1(l, NALL - 1)
                if l == 0:
                    for piece in range(2):
                        copy_mod(piece)
                        copy_turned(piece)
                    act.wait_ge(s_mt.sem, s_mt.at(l, 1))
                    act.wait_ge(s_tA.sem, s_tA.at(l, NALL))
                    for s in range(2):
                        for k in range(HK):
                            h = ht(l)[:, k, s * NX * P:(s + 1) * NX * P]
                            ins = nc.scalar.activation(h, h, ACT.Identity, scale=a1t[:, s, k:k + 1], bias=sht[:, s, k:k + 1])
                        ins.then_inc(s_hmA, 1)
                turning = None
                for n, (kind, i, eng) in enumerate(proj_jobs(l)):
                    if l == 0 and MOD_JOBS.get(n - 1, 0) % 2 == 1:
                        copy_mod(MOD_JOBS[n - 1] // 2)
                        turning = MOD_JOBS[n - 1] // 2 if turned(MOD_JOBS[n - 1] // 2) else None
                    if eng != "A":
                        if turning is not None:
                            copy_turned(turning)
                            turning = None
                        continue
                    act.wait_ge(s_pj.sem, s_pj.at(l, n + 1))
                    bank = pb[n % 4]
                    N = NT[l] * P
                    if kind == "q":
                        ins = nc.scalar.copy(qk[:, i, 0:W_C], bank[:, :])
                    elif kind == "v":
                        ins = nc.scalar.activation(vt[:, i, :], bank[:, 0:W_A], ACT.Gelu_apprx_tanh)
                    elif kind == "c":
                        ins = nc.scalar.copy(cz(l)[:, i, 0:N], bank[:, 0:N])
                    elif kind == "b":
                        ins = nc.scalar.copy(mixt(l)[:, 2 + i, 0:N], bank[:, 0:N])
                    else:
                        ins = nc.scalar.activation(mixt(l)[:, i, 0:N], bank[:, 0:N], ACT.Gelu_apprx_tanh)
                    ins.then_inc(s_pA.sem, 1)
                    if turning is not None:
                        copy_turned(turning)
                        turning = None
                if l == 0:
                    copy_mod(9)
                for t in range(NT[l]):
                    act.wait_ge(s_qtp.sem, s_qtp.at(l, t + 1))
                    nc.scalar.copy(qT[:, :, t * P:(t + 1) * P], pb[4 + 2 * (t % 2)][:, :].rearrange("p (b t) -> p b t", b=4)).then_inc(s_qtA.sem, 1)
                S = steps(l)

                def copy_pt(i):
                    if i >= 0 and pt_engine(i) == "A":
                        n = keys(S[i][0])[1]
                        act.wait_ge(s_pt.sem, s_pt.at(l, i + 1))
                        if i >= 2:
                            act.wait_ge(s_pv.sem, s_pv.at(l, i - 1))
                        nc.scalar.copy(probt(l, i % 2)[:, 0:n // P, :], pb[6 + i % 2][:, 0:n].rearrange("p (k q) -> p k q", q=P)).then_inc(s_ptA.sem, 1)

                def sink_prob(t):
                    act.wait_ge(s_esum.sem, s_esum.at(l, t + 1))
                    nc.scalar.activation(esink[:, :], esum[:, :], ACT.Exp).then_inc(s_es.sem, 1)

                for i, (t, h) in enumerate(S):
                    n = keys(t)[1]
                    act.wait_ge(s_nm.sem, s_nm.at(l, i + 1))
                    if i >= 2:
                        act.wait_ge(s_pt.sem, s_pt.at(l, i - 1))
                    if l == 0 and MOD_STEPS.get(i - 1, 0) % 2 == 1:
                        copy_mod(MOD_STEPS[i - 1] // 2)
                    if h == 1 and t >= 1:
                        sink_prob(t - 1)
                    if t >= 2 and h == 0:
                        act.wait_ge(s_on.sem, s_on.at(l, t - 1))
                    nc.scalar.activation(prob(l, i % 2)[:, 0:n], score_bank(i)[:, 0:n], ACT.Exp, bias=nmx[:, t % 2, h:h + 1],
                                         scale=SCALE, accum_out=rsum[:, t % 2, h:h + 1]).then_inc(s_ex.sem, 1)
                    copy_pt(i - 1)
                copy_pt(len(S) - 1)
                sink_prob(NT[l] - 1)
                for t in range(NT[l]):
                    act.wait_ge(s_ot.sem, s_ot.at(l, t + 1))
                    nc.scalar.copy(mixt(l)[:, 4:8, t * P:(t + 1) * P], pb[2 + t % 2][:, :].rearrange("p (k q) -> p k q", k=4)).then_inc(s_om.sem, 1)
                def quarters(t):
                    act.wait_ge(s_lq.sem, s_lq.at(l, t + 1))
                    if t >= 1:
                        act.wait_ge(s_lg.sem, s_lg.at(l, t))
                    nc.scalar.copy(logit_quarters(l), pb[0][:, 0:P]).then_inc(s_lqc.sem, 1)

                act.wait_ge(s_rw, 32)

                def columns2(t):
                    act.wait_ge(s_h2p.sem, s_h2p.at(l, 2 * t + 1))
                    if t >= 2:
                        act.wait_ge(s_lq.sem, s_lq.at(l, t - 1))
                    nc.scalar.copy(hr(l, t % 2)[:, 0:512], pb[4 + 2 * (t % 2)][:, :]).then_inc(s_h2A.sem, 1)

                for t in range(NT[l]):
                    act.wait_ge(s_ox.sem, s_ox.at(l, NT[l] + t + 1))
                    nc.scalar.activation(h2[:, t, :], xres[:, t, :], ACT.Square, accum_out=st[:, 2, t:t + 1]).then_inc(s_ss2.sem, 1)
                    if t >= 1:
                        columns2(t - 1)
                    if t >= 2:
                        quarters(t - 2)
                quarters(NT[l] - 2)
                nc.scalar.activation(esink[:, 0:1], rbb[:, 0:1], ACT.Sigmoid)
                columns2(NT[l] - 1)
                quarters(NT[l] - 1)
                act.wait_ge(s_lg.sem, s_lg.at(l, NT[l]))
                nc.scalar.activation(work(l, rt0, 16 * NT[l]), pb[1][:, 0:16 * NT[l]], ACT.Sigmoid).then_inc(s_sig.sem, 1)
                act.wait_ge(s_pos.sem, s_pos.at(l, 1))
                total = act.value_load(tab[l][0:1, NE:NE + 1], min_val=NE, max_val=NTILE - 1)
                act.sem_inc(s_y[l], 1)
                act.sem_inc(s_yd[l], 32)
                with act.Fori(0, total) as T:
                    for hf in range(2):
                        act.wait_ge(s_gu[l], T * 2 + (hf + 1))
                        nc.scalar.activation(sg[:, hf * 256:(hf + 1) * 256], pb[hf][0:SLOTS, 0:256], ACT.Silu).then_inc(s_si[l], 1)
                    act.wait_ge(s_d[l], T + 1)
                    act.wait_ge(s_yd[l], T * 32 + 32)
                    nc.scalar.copy(ysb, pb[4][:, :]).then_inc(s_y[l], 1)
                    act.wait_ge(s_y[l], T + 2)
                    for hf in range(2):
                        act.dma_start(ysort[bass.ds(T * SLOTS, SLOTS), hf * 512:(hf + 1) * 512],
                                      ysb[hf * SLOTS:(hf + 1) * SLOTS, :]).then_inc(s_yd[l], 16)
                for t in range(2):
                    scale_low(l, t)
            l = DEPTH - 1
            for t in range(NX):
                act.wait_ge(s_comb.sem, s_comb.at(l, t + 1))
                nc.scalar.activation(hr(l, t), xres[:, t, :], ACT.Square, accum_out=st[:, 0, t:t + 1]).then_inc(s_ssf, 1)

        @block.tensor
        def _(pe):
            pe.wait_ge(s_const, 16)
            pe.wait_ge(s_cvec, 32)
            pe.transpose(pb[0][:, 0:16], work(0, 9216, 128)[0:16, :], ident[0:16, 0:16]).then_inc(s_ctp, 1)

            def modulate(m):
                piece, kh = m // 2, m % 2
                pe.wait_ge(s_wm[m % 4], 16 * (m // 4 + 1))
                if kh == 0 and piece >= 2:
                    pe.wait_ge(s_mr, piece if piece == NP - 1 else piece - 1)
                    pe.wait_ge(s_modtc, n_turned(piece - 1))
                for k in range(HK):
                    for hf in range(2):
                        j = 2 * (k % 2) + hf
                        mm = pe.matmul(mod_bank(piece)[32 * j:32 * j + 32, :], sct[:, kh * HK + k, :],
                                       wmodbuf(m)[:, k, hf * MH:(hf + 1) * MH],
                                       start=(kh == 0 and k < 2), stop=(kh == 1 and k >= HK - 2), tile_position=(0, 32 * j))
                mm.then_inc(s_modpe, 1)

            def turn_mod(piece):
                pe.wait_ge(s_mr, piece + 1)
                R = 64 + 64 * (piece % 2)
                for b in range(MH // P):
                    mm = pe.transpose(mod_bank(piece)[:, b * P:b * P + R], mrow[0:R, b * P:(b + 1) * P], ident[0:R, 0:R])
                mm.then_inc(s_modt, 1)

            for l in range(DEPTH):
                J = proj_jobs(l)

                def turn_small():
                    pe.wait_ge(s_row.sem, s_row.at(l, 64))
                    pe.transpose(pb[2][:, 0:N_ROWS], rows[0:N_ROWS, :], ident[0:N_ROWS, 0:N_ROWS]).then_inc(s_mtp.sem, 1)
                    pe.wait_ge(s_small.sem, s_small.at(l, 96))
                    for h in range(A_GROUPS):
                        mm = pe.transpose(pb[3][:, h * P:(h + 1) * P], ws_raw[:, h, :], ident)
                    mm.then_inc(s_wsp.sem, 1)

                def turn_h1(t):
                    pe.wait_ge(s_hr.sem, s_hr.at(l, t + 1))
                    for hf in range(2):
                        if t >= 2:
                            copied = s_tA if hf == 0 else s_tV
                            pe.wait_ge(copied.sem, copied.at(l, t - 1))
                        for k in range(4):
                            kk = 4 * hf + k
                            mm = pe.transpose(pb[4 + (2 * t + hf) % 4][:, k * P:(k + 1) * P], hr(l, t % 2)[:, kk * P:(kk + 1) * P], ident)
                        mm.then_inc(s_ta.sem, 1)

                def inputs_ready(t):
                    if l == 0:
                        pe.wait_ge(s_hmA, t // NX + 1)
                        pe.wait_ge(s_hmV, t // NX + 1)
                    else:
                        pe.wait_ge(s_tA.sem, s_tA.at(l, t + 1))
                        pe.wait_ge(s_tV.sem, s_tV.at(l, t + 1))

                if l == 0:
                    for t in range(NALL):
                        turn_h1(t)
                    turn_small()
                    pe.wait_ge(s_sct, 1)
                    for m in range(FIRST):
                        modulate(m)
                        if m % 2 == 1:
                            turn_mod(m // 2)
                else:
                    turn_small()
                    turn_h1(0)
                for n, (kind, i, _) in enumerate(J):
                    bank = pb[n % 4]
                    if n == 0:
                        pe.wait_ge(s_mt.sem, s_mt.at(l, 1))
                    if n == 3:
                        pe.wait_ge(s_wst.sem, s_wst.at(l, 1))
                    if kind in ("q", "kv", "v"):
                        inputs_ready(i)
                    elif kind == "c" and i == 0:
                        inputs_ready(NT[l] - 1)
                    pe.wait_ge(s_win[kind].sem, s_win[kind].at(l, 16))
                    if n >= 4:
                        if J[n - 4][2] == "A":
                            pe.wait_ge(s_pA.sem, s_pA.at(l, evacuated(J, n - 3, "A")))
                        else:
                            pe.wait_ge(s_pV.sem, s_pV.at(l, evacuated(J, n - 3, "V")))
                    N = cols_of[kind][1]
                    for k in range(KD):
                        if kind in ("q", "kv", "v"):
                            mm = pe.matmul(bank[:, 0:N], ht(l)[:, k, i * P:(i + 1) * P], win(l, kind)[:, k, :],
                                           start=(k == 0), stop=(k == KD - 1))
                        else:
                            mm = pe.matmul(bank[:, 0:NT[l] * P], win(l, kind)[:, k, i * P:(i + 1) * P],
                                           ht(l)[:, k, 0:NT[l] * P], start=(k == 0), stop=(k == KD - 1))
                    mm.then_inc(s_pj.sem, 1)
                    if l == 0 and MOD_JOBS.get(n - 1, 0) % 2 == 1 and turned(MOD_JOBS[n - 1] // 2):
                        turn_mod(MOD_JOBS[n - 1] // 2)
                    if l > 0 and n < NALL - 1:
                        turn_h1(n + 1)
                    if l == 0 and n in MOD_JOBS:
                        modulate(MOD_JOBS[n])
                if l == 0:
                    pe.wait_ge(s_mr, 10)
                for t in range(NALL):
                    if t < NX:
                        pe.wait_ge(s_rope.sem, s_rope.at(l, t + 1))
                    else:
                        pe.wait_ge(s_pV.sem, s_pV.at(l, NALL))
                        pe.wait_ge(s_pA.sem, s_pA.at(l, min(t + 1, NT[l])))
                    if t >= 2:
                        pe.wait_ge(s_qtA.sem, s_qtA.at(l, min(t - 1, NT[l])))
                        pe.wait_ge(s_qtV.sem, s_qtV.at(l, t - 1))
                    if t < NT[l]:
                        for b in range(4):
                            pe.transpose(pb[4 + 2 * (t % 2)][:, b * P:(b + 1) * P], qk[:, t, b * P:(b + 1) * P], ident)
                    for b in range(2):
                        mm = pe.transpose(pb[5 + 2 * (t % 2)][:, b * P:(b + 1) * P], qk[:, t, W_C + b * P:W_C + (b + 1) * P], ident)
                    mm.then_inc(s_qtp.sem, 1)
                pe.wait_ge(s_vn.sem, s_vn.at(l, NT[l]))
                pe.wait_ge(s_pA.sem, s_pA.at(l, evacuated(J, len(J), "A")))
                pe.wait_ge(s_pV.sem, s_pV.at(l, evacuated(J, len(J), "V")))
                for j in range(2):
                    for t in range(NT[l]):
                        for r in range(2):
                            h = 2 * j + r
                            mm = pe.matmul(pb[j][64 * r:64 * r + 64, t * P:(t + 1) * P], vt[:, t, h * 64:(h + 1) * 64], wst[:, h, :],
                                           start=True, stop=True, tile_position=(0, 64 * r))
                    mm.then_inc(s_gp.sem, 1)
                pe.wait_ge(s_qtA.sem, s_qtA.at(l, NT[l]))
                pe.wait_ge(s_qtV.sem, s_qtV.at(l, NALL))
                S = steps(l)

                def score(i):
                    t, h = S[i]
                    k0, n = keys(t)
                    if i >= 3:
                        pe.wait_ge(s_ex.sem, s_ex.at(l, i - 2))
                    pe.matmul(score_bank(i)[:, 0:n], qT[:, h // 2, t * P:(t + 1) * P], kz[:, h % 2, h // 4, k0:k0 + n],
                              start=True, stop=True).then_inc(s_sc.sem, 1)

                def turn(i):
                    t, h = S[i]
                    n = keys(t)[1]
                    pe.wait_ge(s_ex.sem, s_ex.at(l, i + 1))
                    if i >= 2:
                        e = pt_engine(i - 2)
                        copied = s_ptA if e == "A" else s_ptV
                        pe.wait_ge(copied.sem, copied.at(l, pt_count(i - 2, e)))
                    for k in range(n // P):
                        mm = pe.transpose(pb[6 + i % 2][:, k * P:(k + 1) * P], prob(l, i % 2)[:, k * P:(k + 1) * P], ident)
                    mm.then_inc(s_pt.sem, 1)

                def values(i):
                    t, h = S[i]
                    k0, n = keys(t)
                    e = pt_engine(i)
                    copied = s_ptA if e == "A" else s_ptV
                    pe.wait_ge(copied.sem, copied.at(l, pt_count(i, e)))
                    if i == 0:
                        pe.wait_ge(s_gm.sem, s_gm.at(l, 3))
                    if h == 0 and t >= 2:
                        pe.wait_ge(s_on.sem, s_on.at(l, t - 1))
                    v0 = (h // 4) * HD
                    for k in range(n // P):
                        mm = pe.matmul(pb[t % 2][:, h * HD:(h + 1) * HD], probt(l, i % 2)[:, k, :], vv[:, k0 // P + k, v0:v0 + HD],
                                       start=(k == 0), stop=(k == n // P - 1))
                    mm.then_inc(s_pv.sem, 1)

                def turn_out(t):
                    pe.wait_ge(s_on.sem, s_on.at(l, t + 1))
                    if t >= 2:
                        pe.wait_ge(s_om.sem, s_om.at(l, t - 1))
                    for b in range(4):
                        mm = pe.transpose(pb[2 + t % 2][:, b * P:(b + 1) * P], qk[:, t, b * P:(b + 1) * P], ident)
                    mm.then_inc(s_ot.sem, 1)

                score(0)
                score(1)
                for i in range(len(S)):
                    if i + 2 < len(S):
                        score(i + 2)
                    turn(i)
                    if i >= 1:
                        values(i - 1)
                    if l == 0 and i in MOD_STEPS:
                        modulate(MOD_STEPS[i])
                values(len(S) - 1)
                if l == 0:
                    pe.wait_ge(s_mr, NP)
                for t in range(NT[l]):
                    turn_out(t)
                pe.wait_ge(s_om.sem, s_om.at(l, NT[l]))
                pe.wait_ge(s_gm.sem, s_gm.at(l, 4))
                pe.wait_ge(s_conv.sem, s_conv.at(l, 2))
                def out_job(n):
                    hf, t = n // NT[l], n % NT[l]
                    pe.wait_ge(s_wout[hf].sem, s_wout[hf].at(l, 16))
                    if n >= 2:
                        pe.wait_ge(s_og.sem, s_og.at(l, n - 1))
                    for k in range(KD):
                        mm = pe.matmul(pb[2 + n % 2][:, :], mixt(l)[:, k, t * P:(t + 1) * P], wout(l)[:, hf, k, :],
                                       start=(k == 0), stop=(k == KD - 1))
                    mm.then_inc(s_op.sem, 1)

                def turn_h2(t):
                    pe.wait_ge(s_h2.sem, s_h2.at(l, t + 1))
                    for hf in range(2):
                        if t >= 2:
                            copied = s_h2A if hf == 0 else s_h2V
                            pe.wait_ge(copied.sem, copied.at(l, t - 1))
                        for k in range(4):
                            kk = 4 * hf + k
                            mm = pe.transpose(pb[4 + 2 * (t % 2) + hf][:, k * P:(k + 1) * P], h2[:, t, kk * P:(kk + 1) * P], ident)
                        mm.then_inc(s_h2p.sem, 1)

                def logits(t):
                    pe.wait_ge(s_rw, 32)
                    pe.wait_ge(s_h2A.sem, s_h2A.at(l, t + 1))
                    pe.wait_ge(s_h2V.sem, s_h2V.at(l, t + 1))
                    if t >= 1:
                        pe.wait_ge(s_lqc.sem, s_lqc.at(l, t))
                    for k in range(KD):
                        j = k % 4
                        mm = pe.matmul(pb[0][32 * j:32 * j + NE, 0:P], rwb[:, k, :], hr(l, t % 2)[:, k * P:(k + 1) * P],
                                       start=(k < 4), stop=(k >= 4), tile_position=(0, 32 * j))
                    mm.then_inc(s_lq.sem, 1)

                def fold(t):
                    pe.wait_ge(s_lqc.sem, s_lqc.at(l, t + 1))
                    pe.matmul(pb[1][:, t * NE:(t + 1) * NE], logit_quarters(l), cst[:, C_FOLD:C_FOLD + NE],
                              start=True, stop=True).then_inc(s_lg.sem, 1)

                for n in range(NT[l]):
                    out_job(n)
                for t in range(NT[l]):
                    out_job(NT[l] + t)
                    if t >= 1:
                        turn_h2(t - 1)
                    if t >= 2:
                        logits(t - 2)
                    if t >= 3:
                        fold(t - 3)
                if NT[l] >= 3:
                    fold(NT[l] - 3)
                logits(NT[l] - 2)
                turn_h2(NT[l] - 1)
                fold(NT[l] - 2)
                logits(NT[l] - 1)
                fold(NT[l] - 1)
                pe.wait_ge(s_msk.sem, s_msk.at(l, 1))
                pe.wait_ge(s_rc.sem, s_rc.at(l, 16))
                rc = work(l, 9216, 528)
                W = (NT[l] + 1) * NE
                pe.matmul(pb[1][:, 0:W], rc[:, R_BEFORE:R_BEFORE + P], chosen_experts(l)[:, 0:W], start=True, stop=False)
                for u in range(1, NT[l] + 1):
                    mm = pe.matmul(pb[1][:, u * NE:W], rc[:, R_ONES:R_ONES + P], chosen_experts(l)[:, 0:W - u * NE],
                                   start=False, stop=(u == NT[l]))
                mm.then_inc(s_pre.sem, 1)

                def turn_rows():
                    for k in range(KD):
                        mm = pe.transpose(pb[5][:, k * SLOTS:(k + 1) * SLOTS], hrow[:, k * P:(k + 1) * P], ident[0:SLOTS, 0:SLOTS])
                    mm.then_inc(s_hTp[l], 1)

                def tile(T, n, use):
                    def arrived(part):
                        pe.wait_ge(s_we[n % RING][part], use * 16 + weights_at(l, n % RING, 0))

                    pe.wait_ge(s_hT[l], T + 1)

                    def gate_up(hf, ks):
                        for k in ks:
                            if hf == 0 and k % HK == 0:
                                arrived(2 * (k // HK))
                                arrived(2 * (k // HK) + 1)
                            for r, w in ((0, wgate(n)), (1, wup(n))):
                                mm = pe.matmul(pb[hf][64 * r:64 * r + 64, 0:256], hTe[:, k, :], w[:, k, hf * 256:(hf + 1) * 256],
                                               start=(k == 0), stop=(k == KD - 1), tile_position=(0, 64 * r))
                        if k == KD - 1:
                            mm.then_inc(s_gu[l], 1)

                    def turn_a(hf):
                        pe.wait_ge(s_a[l], T * 2 + (hf + 1))
                        pe.sem_inc(s_passed, 1)
                        for k in range(2):
                            mm = pe.transpose(pb[2 + hf][:, k * SLOTS:(k + 1) * SLOTS], ae[:, (2 * hf + k) * P:(2 * hf + k + 1) * P],
                                              ident[0:SLOTS, 0:SLOTS])
                        mm.then_inc(s_at[l], 1)

                    def down(hf):
                        pe.wait_ge(s_aT[l], T * 2 + (hf + 1))
                        arrived(4 + hf)
                        for k in (2 * hf, 2 * hf + 1):
                            for r in range(2):
                                mm = pe.matmul(pb[4][64 * r:64 * r + 64, :], aTe[:, k, :], wdown(n)[:, k, r * 512:(r + 1) * 512],
                                               start=(k == 0), stop=(k == KF - 1), tile_position=(0, 64 * r))
                        return mm

                    gate_up(0, range(KD))
                    gate_up(1, range(KD // 2))
                    turn_a(0)
                    gate_up(1, range(KD // 2, KD))
                    pe.wait_ge(s_y[l], T + 1)
                    down(0)
                    turn_a(1)
                    pe.wait_ge(s_hrow[l], T * 16 + 16)
                    pe.sem_inc(s_passed, 1)
                    turn_rows()
                    mm = down(1)
                    mm.then_inc(s_d[l], 1)

                def expert(e, use, n):
                    lo = pe.value_load(tab[l][0:1, bass.ds(e, 1)], min_val=0, max_val=NTILE)
                    hi = pe.value_load(tab[l][0:1, bass.ds(e + 1, 1)], min_val=0, max_val=NTILE)
                    with pe.Fori(lo, hi) as T:
                        tile(T, n, use)

                pe.wait_ge(s_pick.sem, s_pick.at(l, 1))
                for k in range(KD):
                    for t in range(NT[l]):
                        mm = pe.matmul(pb[5][:, k * SLOTS:(k + 1) * SLOTS], h2[:, t, k * P:(k + 1) * P], picked[:, t, :],
                                       start=(t == 0), stop=(t == NT[l] - 1))
                mm.then_inc(s_hTp[l], 1)
                pe.wait_ge(s_pos.sem, s_pos.at(l, 1))
                with pe.Fori(0, (NE - 1) // RING) as i:
                    for j in range(RING):
                        expert(i * RING + j, i + 1, l + j)
                expert(NE - 1, (NE - 1) // RING + 1, NE - 1 + l)

        @block.vector
        def _(dve):
            dv = Tally(dve, s_dv)
            link = dv.link
            V = nc.vector

            def rows1(l, t):
                dve.wait_ge(s_r1.sem, s_r1.at(l, t + 1))
                if t >= 2:
                    dve.wait_ge(s_ta.sem, s_ta.at(l, 2 * (t - 1)))
                V.tensor_scalar(hr(l, t % 2), xres[:, t, :], st[:, 1, t:t + 1], None, ALU.mult).then_inc(s_hr.sem, 1)

            def add_mod(piece):
                dve.wait_ge(s_mh, piece + 1)
                a = 64 * (piece % 2)
                V.tensor_tensor(mrow[a:a + 64, :], mrow[a:a + 64, :], mod_bank(piece)[a:a + 64, :], ALU.add).then_inc(s_mr, 1)

            def layer_columns(l):
                dve.wait_ge(s_mtp.sem, s_mtp.at(l, 1))
                link(V.tensor_copy(mt[:, 0:N_ROWS], pb[2][:, 0:N_ROWS]))
                dve.wait_ge(s_wsp.sem, s_wsp.at(l, 1))
                V.tensor_copy(wst[:, :, :], pb[3][:, :].rearrange("p (h q) -> p h q", h=A_GROUPS)).then_inc(s_wst.sem, 1)
                V.tensor_scalar(nsink[:, :], sinkb[:, :], -1.0, None, ALU.mult).then_inc(s_nsink.sem, 1)
                both = lambda a: mt[:, a:a + KD].unsqueeze(1).broadcast_to([P, 2, KD])
                dve.wait_ge(s_modtc, n_turned(6 * l + 2))
                link(V.tensor_tensor(a1s[:, :, :], modt[:, l, 1, :, :], both(MT_BIAS + KD), ALU.add))
                link(V.tensor_tensor(sht[:, :, :], modt[:, l, 0, :, :], both(MT_BIAS), ALU.add))
                V.scalar_tensor_tensor(out=a1t[:, :, :], in0=a1s[:, :, :], scalar=1.0, in1=both(MT_N1),
                                       op0=ALU.add, op1=ALU.mult).then_inc(s_mt.sem, 1)
                dve.wait_ge(s_mt.sem, s_mt.at(l, 1))

            def columns1(l, t):
                dve.wait_ge(s_ta.sem, s_ta.at(l, 2 * t + 2))
                bank, s = pb[4 + (2 * t + 1) % 4], t // NX
                if l == 0:
                    ins = V.tensor_copy(ht(l)[:, HK:KD, t * P:(t + 1) * P], bank[:, :].rearrange("p (k t) -> p k t", k=HK))
                else:
                    for k in range(HK):
                        kk = HK + k
                        ins = V.tensor_scalar(ht(l)[:, kk, t * P:(t + 1) * P], bank[:, k * P:(k + 1) * P],
                                              a1t[:, s, kk:kk + 1], sht[:, s, kk:kk + 1], ALU.mult, ALU.add)
                ins.then_inc(s_tV.sem, 1)

            def combine(l, t):
                dve.wait_ge(s_yg[t].sem, s_yg[t].at(l, 32))
                dve.wait_ge(s_yl.sem, s_yl.at(l, t + 1))
                lo, hi = ybuf2(t, 0), ybuf2(t, 1)
                g2 = vbuf[:, :] if t < NX else ybuf[:, :]
                link(V.scalar_tensor_tensor(out=lo, in0=hi, scalar=wtk[:, 1, t:t + 1], in1=lo, op0=ALU.mult, op1=ALU.add))
                if l + 1 < DEPTH and t % 2 == 1:
                    columns1(l + 1, t // 2)
                link(V.tensor_tensor(lo, lo, g2, ALU.mult))
                V.tensor_tensor(xres[:, t, :], xres[:, t, :], lo, ALU.add).then_inc(s_comb.sem, 1)
                dve.wait_ge(s_comb.sem, s_comb.at(l, t + 1))

            for l in range(DEPTH):
                J = proj_jobs(l)
                N = NT[l] * P
                if l == 0:
                    for t in range(NALL):
                        rows1(l, t)
                        if t >= 1:
                            columns1(l, t - 1)
                    columns1(l, NALL - 1)
                    add_mod(0)
                    add_mod(1)
                    layer_columns(l)
                    dve.wait_ge(s_tV.sem, s_tV.at(l, NALL))
                    for s in range(2):
                        for kk in range(HK, KD):
                            h = ht(l)[:, kk, s * NX * P:(s + 1) * NX * P]
                            ins = V.tensor_scalar(h, h, a1t[:, s, kk:kk + 1], sht[:, s, kk:kk + 1], ALU.mult, ALU.add)
                        ins.then_inc(s_hmV, 1)

                def rope(t):
                    if t < NX:
                        q3 = qk[:, t, :].rearrange("p (h a b c) -> p h a b c", a=2, b=2, c=16)
                        r3 = ropet(l).rearrange("p (h a b c) -> p h a b c", a=2, b=2, c=16)
                        sn = cst[:, C_SIN + t * HD:C_SIN + (t + 1) * HD].rearrange("p (a b c) -> p a b c", a=2, b=2)
                        cs = cst[:, C_COS + t * HD:C_COS + (t + 1) * HD]
                        nh = QW // HD
                        for a in range(2):
                            for b in range(2):
                                ins = V.tensor_tensor(r3[:, :, a, b, :], q3[:, :, a, 1 - b, :],
                                                      sn[:, a, b, :].unsqueeze(1).broadcast_to([P, nh, 16]), ALU.mult)
                        link(ins)
                        qf = qk[:, t, :].rearrange("p (h d) -> p h d", d=HD)
                        link(V.tensor_tensor(qf, qf, cs.unsqueeze(1).broadcast_to([P, nh, HD]), ALU.mult))
                        V.tensor_tensor(qk[:, t, :], qk[:, t, :], ropet(l), ALU.add).then_inc(s_rope.sem, 1)
                        dve.wait_ge(s_rope.sem, s_rope.at(l, t + 1))

                def norm_v(t):
                    link(V.tensor_tensor(yc_flat[:, 0:W_A], vt[:, t, :], vt[:, t, :], ALU.mult))
                    V.tensor_reduce(st[:, 4, t:t + 1], yc_flat[:, 0:W_A], AX, ALU.add).then_inc(s_vs.sem, 1)
                    dve.wait_ge(s_rv.sem, s_rv.at(l, t + 1))
                    V.tensor_scalar(vt[:, t, :], vt[:, t, :], st[:, 5, t:t + 1], None, ALU.mult).then_inc(s_vn.sem, 1)
                    dve.wait_ge(s_vn.sem, s_vn.at(l, t + 1))

                yc_flat = ybuf[:, :]
                kvs = [n for n, j in enumerate(J) if j[0] == "kv"]
                zs = [n for n, j in enumerate(J) if j[0] == "z"]
                if l == 0:
                    add_mod(2)
                    add_mod(3)
                for t, n in enumerate(kvs):
                    dve.wait_ge(s_pj.sem, s_pj.at(l, n + 1))
                    kd = qk[:, t, W_C:W_C + 256].rearrange("p (v r d) -> p v r d", v=NKV, r=2)
                    src = pb[n % 4][:, 0:P].rearrange("p (v d) -> p v d", v=NKV).unsqueeze(2).broadcast_to([P, NKV, 2, HD])
                    V.tensor_copy(kd, src)
                    V.tensor_copy(vv[:, t, :], pb[n % 4][:, P:2 * P]).then_inc(s_pV.sem, 1)
                dve.wait_ge(s_pV.sem, s_pV.at(l, NALL))
                if l == 0:
                    add_mod(4)
                for t in range(NALL):
                    if t < NT[l]:
                        dve.wait_ge(s_pA.sem, s_pA.at(l, t + 1))
                    rope(t)
                for t in range(NT[l]):
                    dve.wait_ge(s_pA.sem, s_pA.at(l, NT[l] + t + 1))
                    norm_v(t)
                if l == 0:
                    add_mod(5)
                    add_mod(6)
                for j, n in enumerate(zs):
                    dve.wait_ge(s_pj.sem, s_pj.at(l, n + 1))
                    dve.wait_ge(s_pA.sem, s_pA.at(l, 2 * NT[l] + j + 1))
                    V.tensor_tensor(cz(l)[:, j, 0:N], pb[n % 4][:, 0:N], cz(l)[:, j, 0:N], ALU.mult).then_inc(s_pV.sem, 1)
                dve.wait_ge(s_pV.sem, s_pV.at(l, NALL + 2))
                if l == 0:
                    for piece in range(7, 10):
                        add_mod(piece)
                for t in range(NALL):
                    dve.wait_ge(s_qtp.sem, s_qtp.at(l, t + 1))
                    if t == 0:
                        dve.wait_ge(s_kz.sem, s_kz.at(l, 1))
                    src = pb[5 + 2 * (t % 2)][:, 0:256].rearrange("p (v t) -> p v t", v=NKV)
                    V.tensor_copy(kz[0:64, 0, :, t * P:(t + 1) * P], src[0:64])
                    V.tensor_copy(kz[64:128, 1, :, t * P:(t + 1) * P], src[64:128]).then_inc(s_qtV.sem, 1)
                for j in range(2):
                    dve.wait_ge(s_gp.sem, s_gp.at(l, j + 1))
                    dve.wait_ge(s_pA.sem, s_pA.at(l, evacuated(J, len(J), "A")))
                    tmp = work(l, 0, 512)
                    g3 = tmp[:, 0:N].rearrange("p (t q) -> p t q", q=P)
                    V.scalar_tensor_tensor(out=g3, in0=pb[j][:, 0:N].rearrange("p (t q) -> p t q", q=P),
                                           scalar=mt[:, MT_GMLP + j:MT_GMLP + j + 1], in1=bsb[:, j, :].unsqueeze(1).broadcast_to([P, NT[l], P]),
                                           op0=ALU.mult, op1=ALU.add).then_inc(s_gm.sem, 1)
                    dve.wait_ge(s_gm.sem, s_gm.at(l, 2 * j + 1))
                    V.tensor_tensor(mixt(l)[:, j, 0:N], mixt(l)[:, j, 0:N], tmp[:, 0:N], ALU.mult).then_inc(s_gm.sem, 1)
                    dve.wait_ge(s_gm.sem, s_gm.at(l, 2 * j + 2))
                def conv_step(n):
                    j, op = n // 4, n % 4
                    w = [mt[:, MT_CONV + 2 * i + j:MT_CONV + 2 * i + j + 1] for i in range(3)]
                    zj = cz(l)[:, j, 0:N].rearrange("p (s t) -> p s t", t=256)
                    yj = yc[:, j, 0:N].rearrange("p (s t) -> p s t", t=256)
                    if op == 0:
                        link(V.tensor_scalar(yj, zj, w[1], None, ALU.mult))
                    elif op == 1:
                        link(V.scalar_tensor_tensor(out=yj[:, :, 1:256], in0=zj[:, :, 0:255], scalar=w[0], in1=yj[:, :, 1:256],
                                                    op0=ALU.mult, op1=ALU.add))
                    elif op == 2:
                        link(V.scalar_tensor_tensor(out=yj[:, :, 0:255], in0=zj[:, :, 1:256], scalar=w[2], in1=yj[:, :, 0:255],
                                                    op0=ALU.mult, op1=ALU.add))
                    else:
                        V.tensor_tensor(mixt(l)[:, 2 + j, 0:N], mixt(l)[:, 2 + j, 0:N], yc[:, j, 0:N], ALU.mult).then_inc(s_conv.sem, 1)

                S = steps(l)
                dve.wait_ge(s_nsink.sem, s_nsink.at(l, 1))

                def copy_pt(i):
                    if i >= 0 and pt_engine(i) == "V":
                        n = keys(S[i][0])[1]
                        dve.wait_ge(s_pt.sem, s_pt.at(l, i + 1))
                        if i >= 2:
                            dve.wait_ge(s_pv.sem, s_pv.at(l, i - 1))
                        V.tensor_copy(probt(l, i % 2)[:, 0:n // P, :], pb[6 + i % 2][:, 0:n].rearrange("p (k q) -> p k q", q=P)).then_inc(s_ptV.sem, 1)

                def normalise(t):
                    dve.wait_ge(s_pv.sem, s_pv.at(l, NH * (t + 1)))
                    dve.wait_ge(s_ex.sem, s_ex.at(l, NH * (t + 1)))
                    dve.wait_ge(s_es.sem, s_es.at(l, t + 1))
                    link(V.tensor_tensor(rden[:, :], rsum[:, t % 2, :], esink[:, :], ALU.add))
                    link(V.reciprocal(rden[:, :], rden[:, :]))
                    o3 = qk[:, t, 0:W_C].rearrange("p (h d) -> p h d", h=NH)
                    V.tensor_tensor(o3, pb[t % 2][:, :].rearrange("p (h d) -> p h d", h=NH),
                                    rden[:, :].unsqueeze(2).broadcast_to([P, NH, HD]), ALU.mult).then_inc(s_on.sem, 1)
                    dve.wait_ge(s_on.sem, s_on.at(l, t + 1))

                for i, (t, h) in enumerate(S):
                    n = keys(t)[1]
                    bank = score_bank(i)
                    dve.wait_ge(s_sc.sem, s_sc.at(l, i + 1))
                    if t < NX:
                        m0 = P if t == 0 else 0
                        link(V.tensor_tensor(bank[:, m0:m0 + P], bank[:, m0:m0 + P], cst[:, C_MASK + t * P:C_MASK + (t + 1) * P], ALU.add))
                    link(V.tensor_reduce(mx[:, h:h + 1], bank[:, 0:n], AX, ALU.max))
                    V.tensor_scalar(nmx[:, t % 2, h:h + 1], mx[:, h:h + 1], -SCALE, nsink[:, h:h + 1], ALU.mult, ALU.min).then_inc(s_nm.sem, 1)
                    if h == NH - 1:
                        dve.wait_ge(s_nm.sem, s_nm.at(l, i + 1))
                        V.tensor_tensor(esum[:, :], sinkb[:, :], nmx[:, t % 2, :], ALU.add).then_inc(s_esum.sem, 1)
                    copy_pt(i - 1)
                    if h == 2 and t >= 1:
                        normalise(t - 1)
                    if 1 <= i <= 8:
                        conv_step(i - 1)
                    if l == 0 and MOD_STEPS.get(i - 1, 0) % 2 == 1:
                        add_mod(MOD_STEPS[i - 1] // 2)
                copy_pt(len(S) - 1)
                normalise(NT[l] - 1)
                dve.wait_ge(s_g1.sem, s_g1.at(l, 16 * (NT[l] // 2)))
                dve.wait_ge(s_a2.sem, s_a2.at(l, 16 * (NT[l] + 1)))
                for s in range(NT[l] // 2):
                    sc2 = scale2(l, s)
                    link(V.scalar_tensor_tensor(out=sc2, in0=sc2, scalar=1.0, in1=vbuf[:, :], op0=ALU.add, op1=ALU.mult))

                def rows2(t):
                    s = t // NX
                    dve.wait_ge(s_r2.sem, s_r2.at(l, t + 1))
                    link(V.scalar_tensor_tensor(out=h2[:, t, :], in0=xres[:, t, :], scalar=st[:, 3, t:t + 1], in1=scale2(l, s),
                                                op0=ALU.mult, op1=ALU.mult))
                    V.tensor_tensor(h2[:, t, :], h2[:, t, :], shift2(l, s), ALU.add).then_inc(s_h2.sem, 1)

                def columns2(t):
                    dve.wait_ge(s_h2p.sem, s_h2p.at(l, 2 * t + 2))
                    if t >= 2:
                        dve.wait_ge(s_lq.sem, s_lq.at(l, t - 1))
                    V.tensor_copy(hr(l, t % 2)[:, 512:1024], pb[5 + 2 * (t % 2)][:, :]).then_inc(s_h2V.sem, 1)

                for hf in range(2):
                    for t in range(NT[l]):
                        s = t // NX
                        g1 = cz(l).rearrange("p j t -> p (j t)") if s == 0 else ybuf[:, :]
                        n = hf * NT[l] + t
                        half = slice(hf * 512, (hf + 1) * 512)
                        tmp = h2[:, t, half]
                        dve.wait_ge(s_op.sem, s_op.at(l, n + 1))
                        V.tensor_tensor(tmp, pb[2 + n % 2][:, :], g1[:, half], ALU.mult).then_inc(s_og.sem, 1)
                        dve.wait_ge(s_og.sem, s_og.at(l, n + 1))
                        V.tensor_tensor(xres[:, t, half], xres[:, t, half], tmp, ALU.add).then_inc(s_ox.sem, 1)
                        dve.wait_ge(s_ox.sem, s_ox.at(l, n + 1))
                        if hf == 1 and t >= 1:
                            columns2(t - 1)
                        if hf == 1:
                            rows2(t)
                columns2(NT[l] - 1)

                T_, B = NT[l], NT[l] * NE // 4
                W = NT[l] * NE
                ra = lambda i, m=64: work(l, rt0 + 64 * i, m)
                score_, sel, kept, gate, posm, himask = (ra(i) for i in range(6))
                chosen = chosen_experts(l)
                cmp_ = ra(8, 256)
                gsum, gone = ra(7)[:, 0:16], ra(7)[:, 16:32]
                nt_e, red = ra(12)[:, 16:32], ra(12)[:, 32:64]
                start_ = ra(13)[:, 0:NE + 1]
                pref = qkbuf[:, 0:(NE + 1) * NE]
                dve.wait_ge(s_rw, 32)
                V.memset(cmp_, 0.0)
                link(V.memset(chosen[:, W:W + NE], 0.0))
                dve.wait_ge(s_sig.sem, s_sig.at(l, 1))
                t3 = lambda ap: ap[:, 0:W].rearrange("p (t e) -> p t e", e=NE)

                def rank(dst, src, nb):
                    c4 = cmp_[:, 0:nb * 16].rearrange("p (b i j) -> p b i j", i=4, j=4)
                    v = src[:, 0:nb * 4].rearrange("p (b j) -> p b j", j=4)
                    for i in range(4):
                        if i > 0:
                            ins = V.tensor_tensor(c4[:, :, i, 0:i], v[:, :, i:i + 1].broadcast_to([P, nb, i]), v[:, :, 0:i], ALU.is_gt)
                        if i < 3:
                            ins = V.tensor_tensor(c4[:, :, i, i + 1:4], v[:, :, i:i + 1].broadcast_to([P, nb, 3 - i]), v[:, :, i + 1:4], ALU.is_ge)
                    link(ins)
                    link(V.tensor_reduce(dst[:, 0:nb * 4].rearrange("p (b j) -> p b j", j=4), c4.rearrange("p b i j -> p b j i"),
                                         AX, ALU.add))

                link(V.tensor_tensor(t3(sel), t3(score_), rbb[:, :].unsqueeze(1).broadcast_to([P, T_, NE]), ALU.add))
                rank(kept, sel, B)
                link(V.scalar_tensor_tensor(out=posm[:, 0:W], in0=kept[:, 0:W], scalar=2.0, in1=sel[:, 0:W], op0=ALU.is_lt, op1=ALU.mult))
                link(V.tensor_reduce(gsum[:, 0:B], posm[:, 0:W].rearrange("p (b j) -> p b j", j=4), AX, ALU.add))
                rank(gone, gsum, T_)
                link(V.tensor_scalar(gone[:, 0:B], gone[:, 0:B], 1.0, None, ALU.is_lt))
                V.scalar_tensor_tensor(out=chosen[:, 0:W].rearrange("p (b j) -> p b j", j=4), in0=kept[:, 0:W].rearrange("p (b j) -> p b j", j=4),
                                       scalar=2.0, in1=gone[:, 0:B].unsqueeze(2).broadcast_to([P, B, 4]),
                                       op0=ALU.is_lt, op1=ALU.mult).then_inc(s_msk.sem, 1)
                dve.wait_ge(s_msk.sem, s_msk.at(l, 1))
                link(V.tensor_tensor(gate[:, 0:W], chosen[:, 0:W], score_[:, 0:W], ALU.mult))
                link(V.tensor_reduce(red[:, 0:T_], t3(gate), AX, ALU.add))
                link(V.reciprocal(red[:, 0:T_], red[:, 0:T_]))
                link(V.tensor_tensor(t3(gate), t3(gate), red[:, 0:T_].unsqueeze(2).broadcast_to([P, T_, NE]), ALU.mult))
                dve.wait_ge(s_pre.sem, s_pre.at(l, 1))
                k8 = cst[:, C_COUNT + 1:C_COUNT + NT[l] * P // SLOTS]
                nk = NT[l] * P // SLOTS - 1
                more = cmp_[:, 0:NE * nk].rearrange("p (e k) -> p e k", k=nk)
                link(V.scalar_tensor_tensor(out=more, in0=k8.unsqueeze(1).broadcast_to([P, NE, nk]), scalar=float(SLOTS),
                                            in1=pb[1][:, W:W + NE].unsqueeze(2).broadcast_to([P, NE, nk]), op0=ALU.mult, op1=ALU.is_lt))
                link(V.tensor_reduce(nt_e, more, AX, ALU.add))
                dve.wait_ge(s_rc.sem, s_rc.at(l, 16))
                pf3 = pref.rearrange("p (a b) -> p a b", b=NE)
                rc3 = work(l, 9216, 528)[:, R_PREFIX:R_PREFIX + (NE + 1) * NE].rearrange("p (a b) -> p a b", b=NE)
                link(V.scalar_tensor_tensor(out=pf3, in0=nt_e.unsqueeze(1).broadcast_to([P, NE + 1, NE]), scalar=1.0, in1=rc3,
                                            op0=ALU.add, op1=ALU.mult))
                link(V.tensor_reduce(start_, pf3, AX, ALU.add))
                V.tensor_copy(tab[l][0:1, 0:NE + 1], start_[0:1, :])
                V.tensor_scalar(tab[l][0:1, NE + 1:NE + 2], start_[0:1, NE:NE + 1], -1.0, float(NTILE), ALU.mult, ALU.add)
                link(V.scalar_tensor_tensor(out=t3(posm), in0=start_[:, 0:NE].unsqueeze(1).broadcast_to([P, T_, NE]), scalar=float(SLOTS),
                                            in1=t3(pb[1][:, :]), op0=ALU.mult, op1=ALU.add))
                link(V.scalar_tensor_tensor(out=posm[:, 0:W], in0=posm[:, 0:W], scalar=1.0, in1=chosen[:, 0:W], op0=ALU.add, op1=ALU.mult))
                link(V.tensor_reduce(posf[:, 1, 0:T_], t3(posm), AX, ALU.max))
                link(V.tensor_reduce(posf[:, 0, 0:T_], t3(posm), AX, ALU.add))
                link(V.tensor_tensor(t3(himask), t3(posm), posf[:, 1, 0:T_].unsqueeze(2).broadcast_to([P, T_, NE]), ALU.is_equal))
                link(V.tensor_tensor(posf[:, 0, 0:T_], posf[:, 0, 0:T_], posf[:, 1, 0:T_], ALU.subtract))
                V.tensor_scalar(posi[:, :, 0:T_], posf[:, :, 0:T_], -1.0, None, ALU.add).then_inc(s_slot.sem, 1)
                dve.wait_ge(s_slot.sem, s_slot.at(l, 1))
                for k in range(2):
                    ins = V.tensor_tensor(same[:, k, 0:T_, :], cst[:, C_COUNT + 1:C_COUNT + 1 + SLOTS].unsqueeze(1).broadcast_to([P, T_, SLOTS]),
                                          posf[:, k, 0:T_].unsqueeze(2).broadcast_to([P, T_, SLOTS]), ALU.is_equal)
                link(ins)
                V.tensor_tensor(picked[:, 0:T_, :], same[:, 0, 0:T_, :], same[:, 1, 0:T_, :], ALU.add).then_inc(s_pick.sem, 1)
                link(V.tensor_tensor(posm[:, 0:W], himask[:, 0:W], gate[:, 0:W], ALU.mult))
                link(V.tensor_tensor(gate[:, 0:W], gate[:, 0:W], posm[:, 0:W], ALU.subtract))
                link(V.tensor_reduce(wtk[:, 1, 0:T_], t3(posm), AX, ALU.add))
                V.tensor_reduce(wtk[:, 0, 0:T_], t3(gate), AX, ALU.add).then_inc(s_pos.sem, 1)

                def copy_rows(count):
                    dve.wait_ge(s_hTp[l], count)
                    V.tensor_copy(hTe, pb[5][:, :].rearrange("p (k s) -> p k s", k=KD)).then_inc(s_hT[l], 1)

                dve.wait_ge(s_pos.sem, s_pos.at(l, 1))
                total = dve.value_load(tab[l][0:1, NE:NE + 1], min_val=NE, max_val=NTILE - 1)
                if l == 0:
                    dve.wait_ge(s_hz, 16 * NTILE)
                copy_rows(1)
                with dve.Fori(0, total) as T:
                    for hf in range(2):
                        dve.wait_ge(s_si[l], T * 2 + (hf + 1))
                        V.tensor_tensor(ae[:, hf * 256:(hf + 1) * 256], sg[:, hf * 256:(hf + 1) * 256], pb[hf][SLOTS:P, 0:256],
                                        ALU.mult).then_inc(s_a[l], 1)
                        dve.wait_ge(s_at[l], T * 2 + (hf + 1))
                        V.tensor_copy(aTe[:, 2 * hf:2 * hf + 2, :], pb[2 + hf][:, 0:2 * SLOTS].rearrange("p (k s) -> p k s", k=2)).then_inc(s_aT[l], 1)
                    copy_rows(T + 2)
                if l + 1 < DEPTH:
                    layer_columns(l + 1)
                dve.wait_ge(s_g2.sem, s_g2.at(l, 16 * (NT[l] // 2)))
                for t in range(NT[l]):
                    combine(l, t)
                    if l + 1 < DEPTH:
                        rows1(l + 1, t)
                if l + 1 < DEPTH:
                    for t in range(2, NALL):
                        columns1(l + 1, t)
            l = DEPTH - 1
            dve.wait_ge(s_fg, 16)
            for t in range(NX):
                dve.wait_ge(s_rf, t + 1)
                V.scalar_tensor_tensor(out=hr(l, t), in0=xres[:, t, :], scalar=st[:, 1, t:t + 1], in1=qtbuf[:, 0:D],
                                       op0=ALU.mult, op1=ALU.mult).then_inc(s_fin, 1)


_INS = ["x", "c", "ctx", "c_ctx", "w_mod", "b_mod", "norm1_g", "norm2_g", "w_in", "gmlp_g", "w_s", "b_s", "conv_w",
        "attn_sink", "w_out", "router_w", "router_b", "w_gate", "w_up", "w_down", "final_g"]
_OUTS = [((1, 256, 1024), "float32")]


def kernel(**inputs):
    import numpy as _np
    import concourse.bacc as _bacc
    from concourse import mybir as _mybir
    from concourse.bass_utils import run_bass_kernel_spmd as _run

    nc = _bacc.Bacc("TRN2", target_bir_lowering=False, num_devices=1)
    given = {name: _np.ascontiguousarray(inputs[name]) for name in _INS}
    given["consts"] = shape_constants(64)
    given["rconsts"] = router_constants(given["router_w"].shape[1])
    arrays, args = {}, []
    for name, a in given.items():
        arrays[f"in_{name}_dram"] = a
        args.append(nc.dram_tensor(f"in_{name}_dram", a.shape, _mybir.dt.from_np(a.dtype), kind="ExternalInput").ap())
    for i, (shape, dtype) in enumerate(_OUTS):
        dt = _mybir.dt.from_np(_np.dtype(dtype))
        args.append(nc.dram_tensor(f"out_{i}_dram", shape, dt, kind="ExternalOutput").ap())
    hybrid_trunk(nc, *args)
    r = _run(nc, [arrays], core_ids=[0])
    got = tuple(r.results[0][f"out_{i}_dram"] for i in range(len(_OUTS)))
    return got[0]
```
